# Optimizing a Trainium2 kernel written in Bass

```python
import math
import jax
import jax.numpy as jnp
from jax import lax
import numpy as np

D_MODEL = 2048
BATCH = 1
SEQ = 256
DEPTH = 1

CHUNK = 64
EPS = 1e-5

SSD_EXPAND = 2
SSD_D_INNER = SSD_EXPAND * D_MODEL
SSD_HEAD_DIM = 64
SSD_HEADS = SSD_D_INNER // SSD_HEAD_DIM
SSD_GROUPS = 8
SSD_HEADS_PER_GROUP = SSD_HEADS // SSD_GROUPS
SSD_STATE = 128
SSD_CONV = 4
SSD_CONV_DIM = SSD_D_INNER + 2 * SSD_GROUPS * SSD_STATE

MLA_HEADS = 16
MLA_Q_RANK = 512
MLA_KV_RANK = 512
MLA_NOPE = 128
MLA_ROPE = 64
MLA_V = 128
MLA_QK = MLA_NOPE + MLA_ROPE
ROPE_THETA = 10000.0
Q_BLOCK = 128

N_BRANCH = 2

PEER_HEADS = 8
PEER_N_KEYS = 128
PEER_EXPERTS = PEER_N_KEYS * PEER_N_KEYS
PEER_TOPK = 16
PEER_D_KEY = 256
PEER_HALF = PEER_D_KEY // 2
PEER_TOKEN_BLOCK = 128

DEEPNORM_ALPHA = (2 * DEPTH) ** 0.25
DEEPNORM_BETA = (8 * DEPTH) ** -0.25

IN_WIDTHS = (SSD_D_INNER, SSD_CONV_DIM, SSD_HEADS, MLA_Q_RANK, MLA_KV_RANK, MLA_ROPE, N_BRANCH * D_MODEL)
IN_DIM = sum(IN_WIDTHS)
IN_OFFSETS = tuple(int(v) for v in np.cumsum(IN_WIDTHS)[:-1])

kernel_name = 'hybrid_ssd_mla_peer_chunk_causal'

def _normalize(x):
    xf = x.astype(jnp.float32)
    xc = xf - jnp.mean(xf, axis=-1, keepdims=True)
    return xc * lax.rsqrt(jnp.mean(xc * xc, axis=-1, keepdims=True) + EPS)

def layer_norm(x):
    return _normalize(x).astype(x.dtype)

def post_layer_norm(x, gain, bias):
    return (_normalize(x) * gain + bias).astype(x.dtype)

def rms_norm(x, gain):
    xf = x.astype(jnp.float32)
    y = xf * lax.rsqrt(jnp.mean(xf * xf, axis=-1, keepdims=True) + EPS)
    return (y * gain).astype(x.dtype)

def rope_tables(positions):
    inv_freq = ROPE_THETA ** (-jnp.arange(0, MLA_ROPE, 2, dtype=jnp.float32) / MLA_ROPE)
    ang = positions.astype(jnp.float32)[..., None] * inv_freq
    return jnp.cos(ang), jnp.sin(ang)

def apply_rope(x, cos, sin):
    x1, x2 = jnp.split(x.astype(jnp.float32), 2, axis=-1)
    return jnp.concatenate([x1 * cos - x2 * sin, x1 * sin + x2 * cos], axis=-1).astype(x.dtype)

def causal_depthwise_conv(x, w, bias):
    y = lax.conv_general_dilated(x, w.astype(x.dtype)[:, None, :], window_strides=(1,),
                                 padding=((SSD_CONV - 1, 0),),
                                 dimension_numbers=('NWC', 'WIO', 'NWC'),
                                 feature_group_count=x.shape[-1])
    return y + bias

def segsum_exp(a):
    cs = jnp.cumsum(a, axis=-1)
    diff = cs[..., :, None] - cs[..., None, :]
    n = a.shape[-1]
    mask = jnp.tril(jnp.ones((n, n), dtype=bool))
    return jnp.exp(jnp.where(mask, diff, -jnp.inf))

def ssd_chunked_scan(xs, dt, a, bm, cm):
    b, s = xs.shape[:2]
    nc = s // CHUNK
    g, hg, p, n = SSD_GROUPS, SSD_HEADS_PER_GROUP, SSD_HEAD_DIM, SSD_STATE
    xdt = (xs.astype(jnp.float32) * dt[..., None]).reshape(b, nc, CHUNK, g, hg, p)
    ad = (dt * a).reshape(b, nc, CHUNK, g, hg).transpose(0, 3, 4, 1, 2)
    bc = bm.astype(jnp.float32).reshape(b, nc, CHUNK, g, n)
    cc = cm.astype(jnp.float32).reshape(b, nc, CHUNK, g, n)
    a_cs = jnp.cumsum(ad, axis=-1)
    decay = segsum_exp(ad)
    cb = jnp.einsum('bclgn,bcsgn->bgcls', cc, bc)
    y_diag = jnp.einsum('bghcls,bcsghp->bclghp', cb[:, :, None] * decay, xdt)
    to_end = jnp.exp(a_cs[..., -1:] - a_cs).transpose(0, 3, 4, 1, 2)
    states = jnp.einsum('bclgn,bclghp->cbghpn', bc, xdt * to_end[..., None])
    chunk_decay = jnp.exp(a_cs[..., -1]).transpose(3, 0, 1, 2)

    def step(carry, inp):
        dec, st = inp
        return carry * dec[..., None, None] + st, carry

    init = jnp.zeros((b, g, hg, p, n), jnp.float32)
    _, prev = lax.scan(step, init, (chunk_decay, states))
    from_start = jnp.exp(a_cs).transpose(0, 3, 4, 1, 2)
    y_off = jnp.einsum('bclgn,cbghpn->bclghp', cc, prev) * from_start[..., None]
    return (y_diag + y_off).reshape(b, s, g * hg, p)

def ssd_branch(z, xbc, dt_raw, conv_w, conv_b, dt_bias, A_log, D_skip, norm_w, w_out):
    b, s, _ = z.shape
    xbc = jax.nn.silu(causal_depthwise_conv(xbc, conv_w, conv_b))
    xs, bm, cm = jnp.split(xbc, (SSD_D_INNER, SSD_D_INNER + SSD_GROUPS * SSD_STATE), axis=-1)
    xs = xs.reshape(b, s, SSD_HEADS, SSD_HEAD_DIM)
    bm = bm.reshape(b, s, SSD_GROUPS, SSD_STATE)
    cm = cm.reshape(b, s, SSD_GROUPS, SSD_STATE)
    dt = jax.nn.softplus(dt_raw.astype(jnp.float32) + dt_bias.astype(jnp.float32))
    a = -jnp.exp(A_log.astype(jnp.float32))
    y = ssd_chunked_scan(xs, dt, a, bm, cm) + xs.astype(jnp.float32) * D_skip.astype(jnp.float32)[:, None]
    yg = (y.reshape(b, s, SSD_D_INNER) * jax.nn.silu(z.astype(jnp.float32))).reshape(
        b, s, SSD_GROUPS, SSD_D_INNER // SSD_GROUPS)
    yg = yg * lax.rsqrt(jnp.mean(yg * yg, axis=-1, keepdims=True) + EPS)
    y = yg.reshape(b, s, SSD_D_INNER) * norm_w
    return jnp.dot(y.astype(z.dtype), w_out)

def chunk_causal_attention(q, k, v):
    b, s, nh, dqk = q.shape
    scale = dqk ** -0.5
    nblk = s // Q_BLOCK
    key_chunk = jnp.arange(s) // CHUNK
    q_blocks = q.reshape(b, nblk, Q_BLOCK, nh, dqk).transpose(1, 0, 2, 3, 4)

    def one_block(args):
        i, q_blk = args
        scores = jnp.einsum('bqhd,bkhd->bhqk', q_blk, k).astype(jnp.float32) * scale
        q_chunk = (i * Q_BLOCK + jnp.arange(Q_BLOCK)) // CHUNK
        mask = key_chunk[None, :] <= q_chunk[:, None]
        probs = jax.nn.softmax(jnp.where(mask, scores, -jnp.inf), axis=-1).astype(v.dtype)
        return jnp.einsum('bhqk,bkhd->bqhd', probs, v)

    out = lax.map(one_block, (jnp.arange(nblk), q_blocks))
    return out.transpose(1, 0, 2, 3, 4).reshape(b, s, nh, v.shape[-1])

def mla_branch(q_a, kv_a, k_r, cos, sin, q_norm_w, w_uq, kv_norm_w, w_ukv, w_o):
    b, s, _ = q_a.shape
    q = jnp.dot(rms_norm(q_a, q_norm_w), w_uq).reshape(b, s, MLA_HEADS, MLA_QK)
    q_nope, q_pe = jnp.split(q, (MLA_NOPE,), axis=-1)
    q_pe = apply_rope(q_pe, cos[:, :, None, :], sin[:, :, None, :])
    kv = jnp.dot(rms_norm(kv_a, kv_norm_w), w_ukv).reshape(b, s, MLA_HEADS, MLA_NOPE + MLA_V)
    k_nope, v = jnp.split(kv, (MLA_NOPE,), axis=-1)
    k_pe = apply_rope(k_r, cos, sin)
    qf = jnp.concatenate([q_nope, q_pe], axis=-1)
    kf = jnp.concatenate([k_nope, jnp.broadcast_to(k_pe[:, :, None, :], (b, s, MLA_HEADS, MLA_ROPE))], axis=-1)
    o = chunk_causal_attention(qf, kf, v)
    return jnp.dot(o.reshape(b, s, MLA_HEADS * MLA_V), w_o)

def peer_ffn(h, w_q, keys_1, keys_2, u_table, v_table):
    b, s, d = h.shape
    q = jnp.dot(h, w_q).reshape(b, s, PEER_HEADS, 2, PEER_HALF)
    s1 = jnp.einsum('bshd,kd->bshk', q[:, :, :, 0], keys_1)
    s2 = jnp.einsum('bshd,kd->bshk', q[:, :, :, 1], keys_2)
    v1, i1 = lax.top_k(s1, PEER_TOPK)
    v2, i2 = lax.top_k(s2, PEER_TOPK)
    n_cand = PEER_TOPK * PEER_TOPK
    cand_score = (v1[..., :, None] + v2[..., None, :]).reshape(b, s, PEER_HEADS, n_cand)
    cand_index = (i1[..., :, None] * PEER_N_KEYS + i2[..., None, :]).reshape(b, s, PEER_HEADS, n_cand)
    top_score, top_pos = lax.top_k(cand_score, PEER_TOPK)
    expert = jnp.take_along_axis(cand_index, top_pos, axis=-1)
    gate = jax.nn.softmax(top_score.astype(jnp.float32), axis=-1).astype(h.dtype)
    n_sel = PEER_HEADS * PEER_TOPK
    nb = (b * s) // PEER_TOKEN_BLOCK

    def block(args):
        h_blk, e_blk, g_blk = args
        u = jnp.take(u_table, e_blk, axis=0)
        act = jax.nn.gelu(jnp.einsum('td,ted->te', h_blk, u), approximate=False)
        v = jnp.take(v_table, e_blk, axis=0)
        return jnp.einsum('te,ted->td', g_blk * act, v)

    out = lax.map(block, (h.reshape(nb, PEER_TOKEN_BLOCK, d),
                          expert.reshape(nb, PEER_TOKEN_BLOCK, n_sel),
                          gate.reshape(nb, PEER_TOKEN_BLOCK, n_sel)))
    return out.reshape(b, s, d)

def hybrid_layer(x, c, cos, sin, w_ada, b_ada, w_in, b_gate, conv_w, conv_b, dt_bias, A_log, D_skip,
                 ssd_norm_w, w_ssd_out, q_norm_w, w_uq, kv_norm_w, w_ukv, w_mla_out, w_mix_out,
                 ln1_g, ln1_b, peer_w_q, peer_keys_1, peer_keys_2, peer_u, peer_v, ln2_g, ln2_b):
    b, s, d = x.shape
    ada = jnp.dot(jax.nn.silu(c), w_ada) + b_ada
    shift1, scale1, gate1, shift2, scale2, gate2 = jnp.split(ada[:, None, :], 6, axis=-1)

    h = layer_norm(x) * (1 + scale1) + shift1
    z, xbc, dt_raw, q_a, kv_a, k_r, g_logits = jnp.split(jnp.dot(h, w_in), IN_OFFSETS, axis=-1)
    y_ssd = ssd_branch(z, xbc, dt_raw, conv_w, conv_b, dt_bias, A_log, D_skip, ssd_norm_w, w_ssd_out)
    y_mla = mla_branch(q_a, kv_a, k_r, cos, sin, q_norm_w, w_uq, kv_norm_w, w_ukv, w_mla_out)
    g = jax.nn.sigmoid((g_logits + b_gate).astype(jnp.float32)).astype(x.dtype).reshape(b, s, N_BRANCH, d)
    mix = jnp.dot(g[:, :, 0] * y_ssd + g[:, :, 1] * y_mla, w_mix_out)
    x = post_layer_norm(DEEPNORM_ALPHA * x + (1 + gate1) * mix, ln1_g, ln1_b)

    h2 = layer_norm(x) * (1 + scale2) + shift2
    f = peer_ffn(h2, peer_w_q, peer_keys_1, peer_keys_2, peer_u, peer_v)
    return post_layer_norm(DEEPNORM_ALPHA * x + (1 + gate2) * f, ln2_g, ln2_b)

def setup_inputs(seed: int = 0) -> dict:
    key = jax.random.key(seed)
    ks = jax.random.split(key, 32)
    L = DEPTH
    f32 = jnp.float32

    def nrm(k, shape, scale):
        return jax.random.normal(k, shape, f32) * scale

    x = nrm(ks[0], (BATCH, SEQ, D_MODEL), 1.0)
    c = nrm(ks[1], (BATCH, D_MODEL), 1.0)
    offset = jax.random.randint(ks[2], (BATCH, 1), 0, 64, dtype=jnp.int32) * CHUNK
    positions = (offset + jnp.arange(SEQ, dtype=jnp.int32)[None, :]).astype(jnp.int32)
    w_ada = nrm(ks[3], (L, D_MODEL, 6 * D_MODEL), 0.25 * D_MODEL ** -0.5)
    b_ada = nrm(ks[4], (L, 6 * D_MODEL), 0.01)
    w_in = nrm(ks[5], (L, D_MODEL, IN_DIM), D_MODEL ** -0.5)
    b_gate = nrm(ks[6], (L, N_BRANCH * D_MODEL), 0.01)
    conv_w = jax.random.uniform(ks[7], (L, SSD_CONV, SSD_CONV_DIM), f32, -1.0, 1.0) * SSD_CONV ** -0.5
    conv_b = nrm(ks[8], (L, SSD_CONV_DIM), 0.01)
    dt0 = jnp.exp(jax.random.uniform(ks[9], (L, SSD_HEADS), f32, math.log(1e-3), math.log(1e-1)))
    dt_bias = dt0 + jnp.log(-jnp.expm1(-dt0))
    A_log = jnp.log(jax.random.uniform(ks[10], (L, SSD_HEADS), f32, 1.0, 16.0))
    D_skip = 1.0 + nrm(ks[11], (L, SSD_HEADS), 0.01)
    ssd_norm_w = 1.0 + nrm(ks[12], (L, SSD_D_INNER), 0.01)
    w_ssd_out = nrm(ks[13], (L, SSD_D_INNER, D_MODEL), SSD_D_INNER ** -0.5)
    q_norm_w = 1.0 + nrm(ks[14], (L, MLA_Q_RANK), 0.01)
    w_uq = nrm(ks[15], (L, MLA_Q_RANK, MLA_HEADS * MLA_QK), MLA_Q_RANK ** -0.5)
    kv_norm_w = 1.0 + nrm(ks[16], (L, MLA_KV_RANK), 0.01)
    w_ukv = nrm(ks[17], (L, MLA_KV_RANK, MLA_HEADS * (MLA_NOPE + MLA_V)), MLA_KV_RANK ** -0.5)
    w_mla_out = nrm(ks[18], (L, MLA_HEADS * MLA_V, D_MODEL), (MLA_HEADS * MLA_V) ** -0.5)
    w_mix_out = nrm(ks[19], (L, D_MODEL, D_MODEL), DEEPNORM_BETA * D_MODEL ** -0.5)
    ln1_g = 1.0 + nrm(ks[20], (L, D_MODEL), 0.01)
    ln1_b = nrm(ks[21], (L, D_MODEL), 0.01)
    peer_w_q = nrm(ks[22], (L, D_MODEL, PEER_HEADS * PEER_D_KEY), D_MODEL ** -0.5)
    peer_keys_1 = nrm(ks[23], (L, PEER_N_KEYS, PEER_HALF), PEER_HALF ** -0.5)
    peer_keys_2 = nrm(ks[24], (L, PEER_N_KEYS, PEER_HALF), PEER_HALF ** -0.5)
    peer_u = nrm(ks[25], (L, PEER_EXPERTS, D_MODEL), D_MODEL ** -0.5)
    peer_v = nrm(ks[26], (L, PEER_EXPERTS, D_MODEL), DEEPNORM_BETA)
    ln2_g = 1.0 + nrm(ks[27], (L, D_MODEL), 0.01)
    ln2_b = nrm(ks[28], (L, D_MODEL), 0.01)
    return {'x': x, 'c': c, 'positions': positions, 'w_ada': w_ada, 'b_ada': b_ada, 'w_in': w_in,
            'b_gate': b_gate, 'conv_w': conv_w, 'conv_b': conv_b, 'dt_bias': dt_bias, 'A_log': A_log,
            'D_skip': D_skip, 'ssd_norm_w': ssd_norm_w, 'w_ssd_out': w_ssd_out, 'q_norm_w': q_norm_w,
            'w_uq': w_uq, 'kv_norm_w': kv_norm_w, 'w_ukv': w_ukv, 'w_mla_out': w_mla_out,
            'w_mix_out': w_mix_out, 'ln1_g': ln1_g, 'ln1_b': ln1_b, 'peer_w_q': peer_w_q,
            'peer_keys_1': peer_keys_1, 'peer_keys_2': peer_keys_2, 'peer_u': peer_u, 'peer_v': peer_v,
            'ln2_g': ln2_g, 'ln2_b': ln2_b}

def reference(x, c, positions, w_ada, b_ada, w_in, b_gate, conv_w, conv_b, dt_bias, A_log, D_skip,
              ssd_norm_w, w_ssd_out, q_norm_w, w_uq, kv_norm_w, w_ukv, w_mla_out, w_mix_out,
              ln1_g, ln1_b, peer_w_q, peer_keys_1, peer_keys_2, peer_u, peer_v, ln2_g, ln2_b):
    cos, sin = rope_tables(positions)
    for l in range(DEPTH):
        x = hybrid_layer(x, c, cos, sin, w_ada[l], b_ada[l], w_in[l], b_gate[l], conv_w[l], conv_b[l],
                         dt_bias[l], A_log[l], D_skip[l], ssd_norm_w[l], w_ssd_out[l], q_norm_w[l],
                         w_uq[l], kv_norm_w[l], w_ukv[l], w_mla_out[l], w_mix_out[l], ln1_g[l], ln1_b[l],
                         peer_w_q[l], peer_keys_1[l], peer_keys_2[l], peer_u[l], peer_v[l],
                         ln2_g[l], ln2_b[l])
    return x


_drawn_inputs = setup_inputs


def setup_inputs(seed=0):
    import zlib

    import numpy as np

    out = dict(_drawn_inputs(seed))
    spreads = {}
    factors = {'b_gate': 7.424,
     'conv_b': 2.674,
     'D_skip': 11.486,
     'ssd_norm_w': 11.697,
     'q_norm_w': 8.0,
     'kv_norm_w': 7.633,
     'ln2_g': 32.173,
     'ln2_b': 30.903}
    for name, (base, spread) in spreads.items():
        noise = np.random.default_rng([zlib.crc32(name.encode()), seed]).standard_normal(out[name].shape)
        drawn = base * np.exp(spread * noise) if base else spread * noise
        out[name] = jnp.asarray(drawn.astype(out[name].dtype))
    for name, factor in factors.items():
        out[name] = (out[name] * factor).astype(out[name].dtype)
    return out
```

```python
import math
from contextlib import ExitStack

import numpy as np

import concourse.bass as bass
from concourse import mybir

F32 = mybir.dt.float32
F32R = mybir.dt.float32r
U32 = mybir.dt.uint32
I32 = mybir.dt.int32
ALU = mybir.AluOpType
ACT = mybir.ActivationFunctionType
AX_X = mybir.AxisListType.X
ds = bass.ds

P = 128
D = 2048
SEQ = 256
BLK = SEQ // P
DC = D // P
EPS = 1e-5
SSD_IN = 2 * D
HEADS = 64
HD = 64
GROUPS = 8
HG = HEADS // GROUPS
CONV_DIM = SSD_IN + 2 * GROUPS * P
CT = CONV_DIM // P
MLA_HEADS = 16
RANK = 512
RC = RANK // P
NOPE, ROPE, MV = 128, 64, 128
PEER_HEADS, KEYS, TOPK = 8, 128, 16
ALPHA = 2 ** 0.25
SCALE = (NOPE + ROPE) ** -0.5
W = 512
SBUF_START = 16384 - 32
QH, KVH = NOPE + ROPE, NOPE + MV
COL_Z = 0
COL_X = SSD_IN
COL_B = COL_X + SSD_IN
COL_C = COL_B + GROUPS * P
COL_DT = SSD_IN + CONV_DIM
COL_QA = COL_DT + HEADS
COL_KVA = COL_QA + RANK
COL_KR = COL_KVA + RANK
COL_G = COL_KR + ROPE

C_ID, C_UP, C_ST, C_ONE, C_MK, C_MQ, C_IOTA, C_FREQ = 0, 128, 256, 384, 512, 768, 896, 912
C_EPS = 944
C_ALL = 945

COLS_T1, COLS_T2 = 120, 248
PC_CW = (0, 48, COLS_T1, COLS_T1 + 48)
PC_C, PC_QN, PC_KVN = 96, 112, 116
PC_NW, PC_CB, PC_BG = COLS_T1 + 96, COLS_T2, COLS_T2 + 48
COLS_ALL = 328

U_ADA1, N_ADA1 = 0, 8
U_LOW = 32
U_ATT, N_ATT = 42, 8
U_MLA, N_MLA = 74, 8
U_SSD, N_SSD = 90, 20
U_G0, N_G0 = 170, 8
U_SO, N_SO = 186, 16
U_ADA2, N_ADA2 = 218, 8
U_MIX, N_MIX = 282, 8
U_WQ, N_WQ = 298, 8
U_END = 314


def constants():
    c = np.zeros((P, C_ALL), np.float32)
    r = np.arange(P)
    c[:, C_ID:C_ID + P] = np.eye(P)
    c[:, C_UP:C_UP + P] = r[:, None] <= r[None, :]
    c[:, C_ST:C_ST + P] = r[:, None] > r[None, :]
    c[:, C_ONE:C_ONE + P] = 1.0
    c[0, C_MK + 192:C_MK + 256] = -1e30
    c[0, C_MQ:C_MQ + 64] = 1.0
    c[:, C_IOTA:C_IOTA + TOPK] = np.arange(TOPK)
    c[:, C_FREQ:C_FREQ + 32] = (10000.0 ** (-np.arange(0, ROPE, 2) / ROPE)).astype(np.float32)
    c[:, C_EPS] = EPS
    return c


class Steps:

    def __init__(self, eng, sem):
        self.eng, self.sem, self.n, self.trips = eng, sem, 0, 0

    def step(self, ins):
        self.n += 1
        ins.then_inc(self.sem, 1)

    def wait(self):
        self.eng.wait_ge(self.sem, self.trips + self.n)

    def link(self, ins):
        self.step(ins)
        self.wait()

    def enter(self, i, per):
        self.trips, self.per, self.at = i * per, per, self.n

    def leave(self, count):
        assert self.n - self.at == self.per, (self.n - self.at, self.per)
        self.n, self.trips = self.at + self.per * count, 0


def build(nc, a, out, stop="all"):
    ctx = ExitStack()
    with ctx:
        KB = 1024

        def at(name, offset, shape, dt=F32):
            return nc.alloc_sbuf_tensor_at(name, shape, dt, offset=SBUF_START + int(offset))

        small = [160]

        def sm(name, shape, dt=F32):
            t = at(name, small[0], shape, dt)
            small[0] += (4 * int(np.prod(shape[1:])) + 31) // 32 * 32
            assert small[0] <= 14 * KB, (name, small[0])
            return t

        def sem(name):
            return ctx.enter_context(nc.semaphore(name))

        con = sm("con", [P, C_ALL])
        cols = sm("cols", [P, COLS_ALL])
        cs2 = sm("cs2", [P, DC, 2], F32R)
        csil = sm("csil", [P, DC])
        adacol = sm("adacol", [P, 2 * DC])
        dtb = sm("dtb", [P, HEADS])
        anegA = sm("anegA", [P, HEADS])
        dskip = sm("dskip", [P, HEADS])
        dtv = sm("dtv", [P, BLK, HEADS])
        adt = sm("adt", [P, BLK, HEADS])
        toend = sm("toend", [P, HEADS])
        fromst = sm("fromst", [P, HEADS])
        cos2 = sm("cos2", [P, BLK, ROPE])
        sin2 = sm("sin2", [P, BLK, ROPE])
        keysT = sm("keysT", [P, 2, KEYS])
        st = sm("st", [P, 64])
        adarow = sm("adarow", [2, 2, W])
        ident = con[:, C_ID:C_ID + P]
        upper = con[:, C_UP:C_UP + P]
        strict = con[:, C_ST:C_ST + P]

        raw = at("raw", 14 * KB, [P, 4, 4, W])
        whi = at("whi", 46 * KB, [P, 2, 4, W], F32R)
        wlo = at("wlo", 62 * KB, [P, 2, 4, W], F32R)

        h_hi = at("h_hi", 78 * KB, [P, DC, SEQ], F32R)
        h_lo = at("h_lo", 94 * KB, [P, DC, SEQ], F32R)
        yT_hi = at("yT_hi", 78 * KB, [P, 2 * DC, SEQ], F32R)
        mx_hi = at("mx_hi", 78 * KB, [P, DC, SEQ], F32R)
        mx_lo = at("mx_lo", 94 * KB, [P, DC, SEQ], F32R)
        h2_hi = at("h2_hi", 78 * KB, [P, DC, SEQ], F32R)
        h2_lo = at("h2_lo", 94 * KB, [P, DC, SEQ], F32R)
        bias2 = at("bias2", 204 * KB, [2, 2, W])
        premix = at("premix", 110 * KB, [P, DC, SEQ])
        h2 = at("h2", 110 * KB, [P, BLK, D])
        x_in = at("x_in", 126 * KB, [P, BLK, D])
        xnT = at("xnT", 142 * KB, [P, DC, SEQ])
        oT = at("oT", 126 * KB, [P, DC, SEQ])
        cqT_hi = at("cqT_hi", 142 * KB, [P, RC, SEQ], F32R)
        cqT_lo = at("cqT_lo", 146 * KB, [P, RC, SEQ], F32R)
        ckT_hi = at("ckT_hi", 150 * KB, [P, RC, SEQ], F32R)
        ckT_lo = at("ckT_lo", 154 * KB, [P, RC, SEQ], F32R)
        y_tok = at("y_tok", 126 * KB, [P, BLK, SSD_IN])
        adabc = at("adabc", 126 * KB, [P, 4, D])
        gate1, shift2, scale2, gate2 = (adabc[:, j, :] for j in range(4))
        rows = at("rows", 158 * KB, [P, 3, P])
        krows = at("krows", 160 * KB, [P, 2, KEYS])
        posi = at("posi", 161 * KB, [P, BLK], I32)
        posf = at("posf", 161 * KB + 32, [P, BLK])
        ang = at("ang", 161 * KB + 64, [P, BLK, 32])
        turn = at("turn", 161 * KB + 512, [P, BLK, 32])
        angs = at("angs", 162 * KB, [P, 2, BLK, 32])
        cn = at("cn", 158 * KB, [P, BLK, RANK])
        junk = at("junk", 162 * KB, [P, RANK])
        sp = [at(f"sp{j}", 166 * KB + 512 * j, [P, BLK, HEADS]) for j in range(6)]
        krt = at("krt", 170 * KB, [P, BLK, ROPE])
        krs = at("krs", 170 * KB + 512, [P, BLK, ROPE])
        kpe2 = at("kpe2", 171 * KB, [P, BLK, 2, ROPE])
        qn = at("qn", 158 * KB, [P, 4, SEQ])
        kn = at("kn", 162 * KB, [P, 4, SEQ])
        vt = at("vt", 166 * KB, [P, BLK, 4 * MV])
        qr = at("qr", 170 * KB, [P, BLK, 4, ROPE])
        qrt = at("qrt", 172 * KB, [P, BLK, 4, ROPE])
        qrs = at("qrs", 174 * KB, [P, BLK, 4, ROPE])
        qpeT = at("qpeT", 176 * KB, [P, 2, SEQ])
        probs = at("probs", 178 * KB, [P, 4, 3 * P])
        pT = at("pT", 184 * KB, [P, 4, 3 * P])
        kpeT = at("kpeT", 190 * KB, [P, SEQ])
        oT_hi = at("oT_hi", 158 * KB, [P, DC, SEQ], F32R)
        oT_lo = at("oT_lo", 174 * KB, [P, DC, SEQ], F32R)
        xc = at("xc", 158 * KB, [P, 4, SEQ])
        bcT = at("bcT", 162 * KB, [P, 2, SEQ])
        x_tok = at("x_tok", 164 * KB, [P, BLK, W])
        xdt = at("xdt", 168 * KB, [P, BLK, W])
        xend = at("xend", 172 * KB, [P, W])
        zs = at("zs", 174 * KB, [P, BLK, W])
        yg = at("yg", 178 * KB, [P, BLK, W])
        rad = at("rad", 182 * KB, [P, 2, 4, P])
        mt = at("mt", 186 * KB, [P, BLK, HG, P])
        cbm = at("cbm", 194 * KB, [P, 3, P])
        yjunk = at("yjunk", 196 * KB, [P, W])
        g0 = at("g0", 192 * KB, [P, DC, SEQ])
        yT_lo = at("yT_lo", 158 * KB, [P, 2 * DC, SEQ], F32R)
        gtmp = at("gtmp", 190 * KB, [P, W])
        x1 = at("x1", 158 * KB, [P, BLK, D])
        ln1 = at("ln1", 174 * KB, [P, 2, D])
        mtmp = at("mtmp", 190 * KB, [P, W])
        qT = at("qT", 192 * KB, [P, DC, SEQ])
        ln2 = at("ln2", 174 * KB, [P, 2, D])
        ROWS = 8
        rrow = at("rrow", 14 * KB, [P, ROWS, D])
        score = at("score", 78 * KB, [P, BLK * PEER_HEADS, 2 * KEYS])
        scur = at("scur", 94 * KB, [P, 2, KEYS])
        swork = at("swork", 95 * KB, [P, 2, KEYS])
        cand = at("cand", 96 * KB, [P, TOPK, TOPK])
        cwork = at("cwork", 97 * KB, [P, TOPK * TOPK])
        onehot = at("onehot", 98 * KB, [P, TOPK, TOPK])
        pk = lambda name, k, shape, dt=F32: at(name, 99 * KB + 256 * k, shape, dt)
        sval = pk("sval", 0, [P, 2, TOPK])
        sidx = pk("sidx", 1, [P, 2, TOPK], U32)
        sidf = pk("sidf", 2, [P, 2, TOPK])
        tpos = pk("tpos", 3, [P, TOPK], U32)
        tab = pk("tab", 4, [P, 2, TOPK], U32)
        tabf = pk("tabf", 5, [P, 2, TOPK])
        tsel = pk("tsel", 6, [P, 2, TOPK])
        tval = pk("tval", 7, [P, 2, TOPK])
        eidf = pk("eidf", 8, [P, TOPK])
        eid = pk("eid", 9, [P, 2, TOPK], U32)
        ngm = pk("ngm", 10, [P, 2])
        gex = pk("gex", 11, [P, 2, TOPK])
        gsum = pk("gsum", 12, [P, 2])
        dots = pk("dots", 13, [P, 2, TOPK])
        gel = pk("gel", 14, [P, 2, TOPK])
        wgt = pk("wgt", 15, [P, 2, TOPK])
        bn = at("bn", 104 * KB, [P, 4, 6])
        fin = at("fin", 192 * KB, [P, D])

        ps = ctx.enter_context(nc.psum_tensor("ps", [P, 2, 2, W], F32))
        aux = ctx.enter_context(nc.psum_tensor("aux", [P, 4, W], F32))
        auxf = aux[:, :, :].rearrange("p b n -> p (b n)")
        psf = ps[:, :, :, :].rearrange("p a b n -> p (a b n)")

        raw_full = [sem(f"raw_full{j}") for j in range(4)]
        hi_ready = sem("hi_ready")
        lo_ready = sem("lo_ready")
        pe_used = sem("pe_used")
        params_in = sem("params_in")
        x_loaded = sem("x_loaded")
        bias_in = [sem(f"bias_in{j}") for j in range(2)]
        zeroed = sem("zeroed")
        rows_turned = sem("rows_turned")
        cols_ready = sem("cols_ready")
        c_hi_ready = sem("c_hi_ready")
        c_ready = sem("c_ready")
        x_normed = sem("x_normed")
        x_turned = sem("x_turned")
        xT_ready = sem("xT_ready")
        adarow_ready = sem("adarow_ready")
        ada_turned = sem("ada_turned")
        ada_read = sem("ada_read")
        angles_ready = sem("angles_ready")
        sines_ready = sem("sines_ready")
        h_full = sem("h_full")
        h_hi_ready = sem("h_hi_ready")
        h_ready = sem("h_ready")
        sumsq_ready = sem("sumsq_ready")
        cn_ready = sem("cn_ready")
        cn_turned = sem("cn_turned")
        cn_hi_ready = sem("cn_hi_ready")
        cn_split = sem("cn_split")
        sp_x = sem("sp_x")
        sp_e = sem("sp_e")
        neg_a = sem("neg_a")
        adt_ready = sem("adt_ready")
        cum_ready = sem("cum_ready")
        decay_ready = sem("decay_ready")
        kpe_ready = sem("kpe_ready")
        kpe_turned = sem("kpe_turned")
        kpe_read = sem("kpe_read")
        att_evac_a = sem("att_evac_a")
        att_evac_v = sem("att_evac_v")
        qr_copied = sem("qr_copied")
        qr_ready = sem("qr_ready")
        qpe_turned = sem("qpe_turned")
        qpe_read = sem("qpe_read")
        scores_done = sem("scores_done")
        negmax_ready = sem("negmax_ready")
        exp_done = sem("exp_done")
        probs_ready = sem("probs_ready")
        probs_turned = sem("probs_turned")
        pT_a = sem("pT_a")
        pT_v = sem("pT_v")
        pv_done = sem("pv_done")
        o_read = sem("o_read")
        o_hi_ready = sem("o_hi_ready")
        o_split = sem("o_split")
        b_free = sem("b_free")
        conv_done = sem("conv_done")
        silu_done = sem("silu_done")
        xt_turned = sem("xt_turned")
        xt_ready = sem("xt_ready")
        xdt_ready = sem("xdt_ready")
        xskip_ready = sem("xskip_ready")
        rad_ready = sem("rad_ready")
        cb_done = sem("cb_done")
        cb_read = sem("cb_read")
        diff_done = sem("diff_done")
        decay_exp = sem("decay_exp")
        mt_ready = sem("mt_ready")
        y_done = sem("y_done")
        z_silu = sem("z_silu")
        yg_ready = sem("yg_ready")
        ysq_ready = sem("ysq_ready")
        ytok_ready = sem("ytok_ready")
        g0_ready = sem("g0_ready")
        yt_turned = sem("yt_turned")
        yt_hi = sem("yt_hi")
        yt_split = sem("yt_split")
        premix_ready = sem("premix_ready")
        mx_hi_ready = sem("mx_hi_ready")
        mx_split = sem("mx_split")
        res_in = sem("res_in")
        bc_turned = sem("bc_turned")
        bc_read = sem("bc_read")
        h2_ready = sem("h2_ready")
        h2_turned = sem("h2_turned")
        h2_hi_ready = sem("h2_hi_ready")
        h2_split = sem("h2_split")
        qT_a = sem("qT_a")
        qT_v = sem("qT_v")
        score_done = sem("score_done")
        score_a = sem("score_a")
        score_v = sem("score_v")
        h2_psum = sem("h2_psum")
        ln2_in = sem("ln2_in")
        expert_ready = sem("expert_ready")
        top_ready = sem("top_ready")
        gate_exp = sem("gate_exp")
        gelu_ready = sem("gelu_ready")
        row_full = [sem(f"row_full{j}") for j in range(ROWS)]
        row_used = sem("row_used")
        var_ready = sem("var_ready")
        std_ready = sem("std_ready")
        fin_ready = sem("fin_ready")
        out_done = sem("out_done")
        held = sem("held")
        dve_step = sem("dve_step")
        act_step = sem("act_step")
        pool_step = sem("pool_step")
        probe_done = sem("probe_done")

        def kview(w):
            return w[0].rearrange("(kc p) n -> p kc n", p=P)

        w_ada, w_in = kview(a["w_ada"]), kview(a["w_in"])
        w_uq, w_ukv = kview(a["w_uq"]), kview(a["w_ukv"])
        w_so, w_mo = kview(a["w_ssd_out"]), kview(a["w_mla_out"])
        w_mix, w_pq = kview(a["w_mix_out"]), kview(a["peer_w_q"])

        order = ["setup", "low", "att", "mla", "ssd", "g0", "yt", "so", "ada2", "mix", "h2", "wq", "all"]
        upto = order.index(stop)

        def on(phase):
            return order.index(phase) <= upto

        last_unit = {"setup": U_LOW, "low": U_ATT, "att": U_MLA, "mla": U_SSD, "ssd": U_G0, "g0": U_SO, "yt": U_SO,
                     "so": U_ADA2, "ada2": U_MIX, "mix": U_WQ, "h2": U_WQ, "wq": U_END, "all": U_END}[stop]

        def full_count(base, j, i, per):
            return 16 * ((base + j) // 4 + 1) + i * (16 * (per // 4))

        block = ctx.enter_context(nc.Block())

        @block.sync
        def _(sp_):
            def load(base, j, i, per, src):
                n = base + j
                sp_.wait_ge(lo_ready, i * per + (n + 1))
                sp_.sem_inc(held, 1)
                kcs, width = src.shape[1:]
                dst = raw[:, n % 4, :, 0:width] if kcs == 4 else \
                    raw[:, n % 4].rearrange("p a b -> p (a b)")[:, 0:kcs * width].rearrange(
                        "p (kc n) -> p kc n", kc=kcs)
                sp_.dma_start(dst, src).then_inc(raw_full[n % 4], 16)

            def small_in(dst, src):
                sp_.dma_start(dst, src).then_inc(params_in, 16)

            def rowsof(ap, first, n):
                return ap.rearrange("a (r p) -> (a r) p", p=P)[first:first + n, :]

            small_in(rows[PC_C:PC_C + DC, 0, :], rowsof(a["c"], 0, DC))
            for j in range(4):
                small_in(rows[48 * (j % 2):48 * (j % 2) + 48, j // 2, :], rowsof(a["conv_w"][0], j * CT, CT))
            small_in(rows[PC_QN:PC_QN + RC, 0, :], rowsof(a["q_norm_w"], 0, RC))
            small_in(rows[PC_KVN:PC_KVN + RC, 0, :], rowsof(a["kv_norm_w"], 0, RC))
            small_in(rows[96:96 + 2 * DC, 1, :], rowsof(a["ssd_norm_w"], 0, 2 * DC))
            small_in(rows[0:CT, 2, :], rowsof(a["conv_b"], 0, CT))
            small_in(rows[CT:CT + 2 * DC, 2, :], rowsof(a["b_gate"], 0, 2 * DC))
            small_in(con[:, :], a["consts"])
            small_in(krows[:, 0, :], a["peer_keys_1"][0])
            small_in(krows[:, 1, :], a["peer_keys_2"][0])
            with nc.allow_non_contiguous_dma(reason="256 positions, one for each token"):
                small_in(posi[:, :], a["positions"].rearrange("b (t p) -> p (b t)", p=P))
            small_in(dtb[:, :], a["dt_bias"].broadcast_to([P, HEADS]))
            small_in(anegA[:, :], a["A_log"].broadcast_to([P, HEADS]))
            small_in(dskip[:, :], a["D_skip"].broadcast_to([P, HEADS]))
            for b in range(BLK):
                sp_.dma_start(x_in[:, b, :], a["x"][0, b * P:(b + 1) * P, :]).then_inc(x_loaded, 16)

            def ada_slab(base, j, i, first_slab, slot):
                for q in range(4):
                    load(base, 4 * j + q, i, 8, w_ada[:, 4 * q:4 * q + 4, ds(i * 2 * W + (first_slab + slot) * W, W)])

            with sp_.Fori(0, 4) as i:
                for j in range(2):
                    ada_slab(U_ADA1, j, i, 0, j)
            if on("low"):
                for s, col in enumerate((COL_QA, COL_KVA)):
                    for q in range(4):
                        load(U_LOW, 4 * s + q, 0, 0, w_in[:, 4 * q:4 * q + 4, col:col + W])
                for k, col in enumerate((COL_DT, COL_KR)):
                    load(U_LOW, 8 + k, 0, 0, w_in[:, :, col:col + 64])
            if on("att"):
                with sp_.Fori(0, 4) as i:
                    for k in range(2):
                        load(U_ATT, k, i, N_ATT, w_uq[:, :, ds(i * 4 * QH + k * 2 * QH, 2 * QH)])
                    for k in range(2):
                        load(U_ATT, 2 + k, i, N_ATT, w_ukv[:, :, ds(i * 4 * KVH + k * 2 * KVH, 2 * KVH)])
                    for q in range(4):
                        load(U_ATT, 4 + q, i, N_ATT, w_in[:, 4 * q:4 * q + 4, ds(i * W + (COL_G + D), W)])
            if on("mla"):
                with sp_.Fori(0, 2) as i:
                    for u in range(8):
                        load(U_MLA, u, i, N_MLA, w_mo[:, 4 * (u % 4):4 * (u % 4) + 4, ds(i * 2 * W + (u // 4) * W, W)])
            if on("ssd"):
                with sp_.Fori(0, 4) as i:
                    for g in range(2):
                        for q in range(4):
                            load(U_SSD, 10 * g + q, i, N_SSD,
                                 w_in[:, 4 * q:4 * q + 4, ds(i * 2 * W + (COL_X + g * W), W)])
                        for k, col in enumerate((COL_B, COL_C)):
                            load(U_SSD, 10 * g + 4 + k, i, N_SSD, w_in[:, :, ds(i * 2 * P + (col + g * P), P)])
                        for q in range(4):
                            load(U_SSD, 10 * g + 6 + q, i, N_SSD,
                                 w_in[:, 4 * q:4 * q + 4, ds(i * 2 * W + (COL_Z + g * W), W)])
            if on("g0"):
                with sp_.Fori(0, 2) as i:
                    for u in range(8):
                        load(U_G0, u, i, N_G0,
                             w_in[:, 4 * (u % 4):4 * (u % 4) + 4, ds(i * 2 * W + COL_G + (u // 4) * W, W)])
            if on("so"):
                with sp_.Fori(0, 2) as i:
                    for u in range(16):
                        load(U_SO, u, i, N_SO,
                             w_so[:, 4 * (u % 8):4 * (u % 8) + 4, ds(i * 2 * W + (u // 8) * W, W)])
            if on("ada2"):
                with sp_.Fori(0, 8) as i:
                    for j in range(2):
                        ada_slab(U_ADA2, j, i, 8, j)
            if on("mix"):
                with sp_.Fori(0, 2) as i:
                    for u in range(8):
                        load(U_MIX, u, i, N_MIX, w_mix[:, 4 * (u % 4):4 * (u % 4) + 4, ds(i * 2 * W + (u // 4) * W, W)])
            if on("wq"):
                with sp_.Fori(0, 2) as i:
                    for u in range(8):
                        load(U_WQ, u, i, N_WQ, w_pq[:, 4 * (u % 4):4 * (u % 4) + 4, ds(i * 2 * W + (u // 4) * W, W)])
            if not on("wq"):
                load(last_unit, 0, 0, 0, w_in[:, 0:4, 0:W])
            if on("all"):
                for b in range(BLK):
                    sp_.wait_ge(fin_ready, b + 1)
                    sp_.dma_start(out[0, b * P:(b + 1) * P, :], fin[:, :]).then_inc(out_done, 16)
                sp_.wait_ge(out_done, 16 * BLK)

        @block.tensor
        def _(pe):
            mm = nc.tensor.matmul

            def wait_unit(base, j, i, per):
                pe.wait_ge(lo_ready, i * per + (base + j + 5))

            def token_unit(base, j, i, per, x_hi, x_lo, k0, klast, outs, width=W, kcs=4, used=True):
                wait_unit(base, j, i, per)
                n = (base + j) % 2
                hi, lo = whi[:, n], wlo[:, n]
                if kcs != 4:
                    hi, lo = (w.rearrange("p a b -> p (a b)")[:, 0:kcs * width].rearrange(
                        "p (kc n) -> p kc n", kc=kcs) for w in (hi, lo))
                for kc in range(kcs):
                    k = k0 + kc
                    for b in range(BLK):
                        t = slice(b * P, b * P + P)
                        mm(outs[b], x_hi[:, k, t], hi[:, kc, 0:width], start=(k == 0), stop=False)
                        mm(outs[b], x_lo[:, k, t], hi[:, kc, 0:width], start=False, stop=False)
                        last = mm(outs[b], x_hi[:, k, t], lo[:, kc, 0:width], start=False, stop=(k == klast))
                if used:
                    last.then_inc(pe_used, 1)

            def channel_unit(base, j, i, per, x_hi, x_lo, k0, klast, tiles, kcs=4, used=True):
                wait_unit(base, j, i, per)
                n = (base + j) % 2
                hi, lo = whi[:, n], wlo[:, n]
                if kcs != 4:
                    hi, lo = (w.rearrange("p a b -> p (a b)").rearrange("p (kc n) -> p kc n", kc=kcs)
                              for w in (hi, lo))
                for kc in range(kcs):
                    k = k0 + kc
                    for o, c, first in tiles:
                        wh, wl = hi[:, kc, c:c + P], lo[:, kc, c:c + P]
                        mm(o, wh, x_hi[:, k, :], start=(k == 0 and first), stop=False, skip_group_check=True)
                        mm(o, wh, x_lo[:, k, :], start=False, stop=False, skip_group_check=True)
                        last = mm(o, wl, x_hi[:, k, :], start=False, stop=(k == klast), skip_group_check=True)
                if used:
                    last.then_inc(pe_used, 1)

            def slab_tiles(buf):
                return [(ps[:, buf, t // 2, (t % 2) * SEQ:(t % 2) * SEQ + SEQ], t * P, t % 2 == 0) for t in range(4)]

            pe.sem_inc(pe_used, 2)
            pe.sem_inc(diff_done, 2)

            pe.wait_ge(params_in, 16 * 17)
            for j, (first, n) in enumerate(((0, COLS_T1), (COLS_T1, P), (COLS_T2, COLS_ALL - COLS_T2))):
                last = nc.tensor.transpose(aux[:, 0, first:first + n], rows[0:n, j, :], ident[0:n, 0:n])
            last.then_inc(rows_turned, 1)
            for j in range(2):
                last = nc.tensor.transpose(aux[:, 1, j * P:j * P + P], krows[:, j, :], ident)
            last.then_inc(rows_turned, 1)
            pe.wait_ge(x_normed, BLK)
            pe.wait_ge(cols_ready, 2)
            for r in range(4):
                if r >= 2:
                    pe.wait_ge(xT_ready, r - 1)
                for k in range(4):
                    for b in range(BLK):
                        last = nc.tensor.transpose(
                            aux[:, 2 * (r % 2) + k // 2, (k % 2) * SEQ + b * P:(k % 2) * SEQ + b * P + P],
                            x_in[:, b, (4 * r + k) * P:(4 * r + k) * P + P], ident)
                last.then_inc(x_turned, 1)
            pe.wait_ge(xT_ready, 4)
            pe.wait_ge(c_ready, 1)

            def ada_slab(base, i, slot, buf):
                for q in range(4):
                    wait_unit(base, 4 * slot + q, i, 8)
                    n = (base + 4 * slot + q) % 2
                    for kc in range(4):
                        k = 4 * q + kc
                        mm(ps[0:2, buf, 0, :], cs2[:, k, :], whi[:, n, kc, :], start=(k == 0), stop=False)
                        last = mm(ps[0:2, buf, 0, :], cs2[:, k, :], wlo[:, n, kc, :], start=False, stop=(k == DC - 1))
                    last.then_inc(pe_used, 1)

            with pe.Fori(0, 4) as i:
                for j in range(2):
                    ada_slab(U_ADA1, i, j, j)
                    pe.wait_ge(adarow_ready, i * 2 + (j + 3))
                    for t in range(4):
                        last = mm(aux[:, 3, 4 * j + t:4 * j + t + 1], adarow[:, j, t * P:t * P + P],
                                  con[0:2, C_ONE:C_ONE + 1], start=True, stop=True)
                    last.then_inc(ada_turned, 1)
            if on("low"):
                pe.wait_ge(h_ready, 4)
                for s in range(2):
                    for q in range(4):
                        token_unit(U_LOW, 4 * s + q, 0, 0, h_hi, h_lo, 4 * q, DC - 1,
                                   [ps[:, s, b, :] for b in range(BLK)])

                def turn_cn(s):
                    pe.wait_ge(cn_ready, s + 1)
                    for t in range(RC):
                        for b in range(BLK):
                            last = nc.tensor.transpose(
                                aux[:, 2 * s + t // 2, (t % 2) * SEQ + b * P:(t % 2) * SEQ + b * P + P],
                                cn[:, b, t * P:t * P + P], ident)
                    last.then_inc(cn_turned, 1)

                turn_cn(0)
                for k in range(2):
                    token_unit(U_LOW, 8 + k, 0, 0, h_hi, h_lo, 0, DC - 1,
                               [ps[:, 0, b, 64 * k:64 * k + 64] for b in range(BLK)], width=64, kcs=DC)
                turn_cn(1)
                pe.wait_ge(adt_ready, 1)
                pe.wait_ge(cn_split, 1)
                mm(aux[:, 0, 0:HEADS], strict, adt[:, 0, :], start=True, stop=True)
                mm(aux[:, 0, HEADS:2 * HEADS], upper, adt[:, 1, :], start=True, stop=True).then_inc(cum_ready, 1)
                pe.wait_ge(kpe_ready, 1)
                for b in range(BLK):
                    last = nc.tensor.transpose(aux[:, 1, b * P:b * P + P],
                                               kpe2[:, b, :, :].rearrange("p a b -> p (a b)"), ident)
                last.then_inc(kpe_turned, 1)
            if on("att"):
                pe.wait_ge(cn_split, 2)
                pe.wait_ge(kpe_read, 1)
                pe.wait_ge(decay_ready, 1)
                with pe.Fori(0, 4) as i:
                    for k in range(2):
                        channel_unit(U_ATT, k, i, N_ATT, cqT_hi, cqT_lo, 0, RC - 1,
                                     [(ps[:, 1, k, e * SEQ:e * SEQ + SEQ], e * QH, e == 0) for e in range(2)], used=False)
                        if k == 0:
                            pe.wait_ge(b_free, i + 1)
                        n = (U_ATT + k) % 2
                        rope = [w[:, n, :, 0:2 * QH].rearrange("p kc (e m) -> p kc e m", e=2)[:, :, :, NOPE:QH]
                                for w in (whi, wlo)]
                        for b in range(BLK):
                            o = ps[:, 0, 0, b * 256 + k * P:b * 256 + k * P + P]
                            t = slice(b * P, b * P + P)
                            for kc in range(RC):
                                mm(o, cqT_hi[:, kc, t], rope[0][:, kc], start=(kc == 0), stop=False)
                                mm(o, cqT_lo[:, kc, t], rope[0][:, kc], start=False, stop=False)
                                last = mm(o, cqT_hi[:, kc, t], rope[1][:, kc], start=False, stop=(kc == RC - 1))
                        last.then_inc(pe_used, 1)
                    for k in range(2):
                        channel_unit(U_ATT, 2 + k, i, N_ATT, ckT_hi, ckT_lo, 0, RC - 1,
                                     [(aux[:, 2 + k, e * SEQ:e * SEQ + SEQ], e * KVH, e == 0) for e in range(2)],
                                     used=False)
                        n = (U_ATT + 2 + k) % 2
                        val = [w[:, n, :, :].rearrange("p kc (e m) -> p kc e m", e=2)[:, :, :, NOPE:KVH]
                               for w in (whi, wlo)]
                        for b in range(BLK):
                            o = aux[:, b, k * 256:k * 256 + 256]
                            t = slice(b * P, b * P + P)
                            for kc in range(RC):
                                mm(o, ckT_hi[:, kc, t], val[0][:, kc], start=(kc == 0), stop=False)
                                mm(o, ckT_lo[:, kc, t], val[0][:, kc], start=False, stop=False)
                                last = mm(o, ckT_hi[:, kc, t], val[1][:, kc], start=False, stop=(kc == RC - 1))
                        last.then_inc(pe_used, 1)
                    channel_unit(U_ATT, 4, i, N_ATT, h_hi, h_lo, 0, DC - 1, slab_tiles(0))
                    pe.wait_ge(att_evac_a, i + 1)
                    pe.wait_ge(att_evac_v, i + 1)
                    pe.wait_ge(qr_ready, i + 1)
                    for pair in range(2):
                        for b in range(BLK):
                            last = nc.tensor.transpose(
                                aux[:, 2, pair * SEQ + b * P:pair * SEQ + b * P + P],
                                qr[:, b, 2 * pair:2 * pair + 2, :].rearrange("p a b -> p (a b)"), ident)
                    last.then_inc(qpe_turned, 1)
                    channel_unit(U_ATT, 5, i, N_ATT, h_hi, h_lo, 4, DC - 1, slab_tiles(0))
                    pe.wait_ge(qpe_read, i + 1)
                    for h in range(4):
                        r = slice(64 * (h % 2), 64 * (h % 2) + 64)
                        for b in range(BLK):
                            nk = P * (b + 1)
                            o = aux[:, h, b * P:b * P + nk]
                            t = slice(b * P, b * P + P)
                            mm(o, qn[:, h, t], kn[:, h, 0:nk], start=True, stop=False)
                            mm(o, qpeT[r, h // 2, t], kpeT[r, 0:nk], start=False, stop=False)
                            last = mm(o, con[0:1, C_MQ:C_MQ + P], con[0:1, C_MK + 256 - nk:C_MK + 256],
                                      start=False, stop=True)
                    last.then_inc(scores_done, 1)
                    channel_unit(U_ATT, 6, i, N_ATT, h_hi, h_lo, 8, DC - 1, slab_tiles(0))
                    channel_unit(U_ATT, 7, i, N_ATT, h_hi, h_lo, 12, DC - 1, slab_tiles(0))
                    pe.wait_ge(probs_ready, i + 1)
                    for h in range(4):
                        for k in range(3):
                            last = nc.tensor.transpose(aux[:, h, k * P:k * P + P], probs[:, h, k * P:k * P + P], ident)
                        last.then_inc(probs_turned, 1)
                    for h in range(4):
                        pe.wait_ge(pT_v if h % 2 else pT_a, i * 2 + (h // 2 + 1))
                        v0, v1 = (vt[:, b, h * MV:h * MV + MV] for b in range(BLK))
                        mm(aux[:, h, 0:P], v0, pT[:, h, 0:P], start=True, stop=True)
                        mm(aux[:, h, P:2 * P], v0, pT[:, h, P:2 * P], start=True, stop=False)
                        last = mm(aux[:, h, P:2 * P], v1, pT[:, h, 2 * P:3 * P], start=False, stop=True)
                    last.then_inc(pv_done, 1)
            if on("mla"):
                pe.wait_ge(o_split, 4)
                with pe.Fori(0, 2) as i:
                    for s in range(2):
                        for q in range(4):
                            channel_unit(U_MLA, 4 * s + q, i, N_MLA, oT_hi, oT_lo, 4 * q, DC - 1, slab_tiles(1 - s))
            if on("ssd"):
                with pe.Fori(0, 4) as i:
                    for g in range(2):
                        u, bx, bb = 10 * g, 1 - g, g
                        grp = i * 2 + g
                        for q in range(4):
                            channel_unit(U_SSD, u + q, i, N_SSD, h_hi, h_lo, 4 * q, DC - 1, slab_tiles(bx))
                        for k in range(2):
                            channel_unit(U_SSD, u + 4 + k, i, N_SSD, h_hi, h_lo, 0, DC - 1,
                                         [(ps[:, bb, k, 0:SEQ], 0, True)], kcs=DC)
                        zout = [ps[:, bx, b, :] for b in range(BLK)]
                        token_unit(U_SSD, u + 6, i, N_SSD, h_hi, h_lo, 0, DC - 1, zout)
                        pe.wait_ge(silu_done, grp * 5 + 4)
                        for t in range(4):
                            for b in range(BLK):
                                last = nc.tensor.transpose(aux[:, b, t * P:t * P + P], xc[:, t, b * P:b * P + P], ident)
                        last.then_inc(xt_turned, 1)
                        token_unit(U_SSD, u + 7, i, N_SSD, h_hi, h_lo, 4, DC - 1, zout)
                        pe.wait_ge(silu_done, grp * 5 + 5)
                        for k, (s, l) in enumerate(((0, 0), (1, 1), (0, 1))):
                            last = mm(aux[:, 2, k * P:k * P + P], bcT[:, 0, s * P:s * P + P],
                                      bcT[:, 1, l * P:l * P + P], start=True, stop=True)
                        last.then_inc(cb_done, 1)
                        for k in range(4):
                            pe.wait_ge(rad_ready, grp * 4 + (k + 1))
                            if k == 1:
                                pe.wait_ge(cb_read, grp + 1)
                            if k >= 2:
                                pe.wait_ge(decay_exp, grp * 4 + (k - 1))
                            mm(aux[:, 3 - k % 2, :], strict, rad[:, k % 2, :, :].rearrange("p h l -> p (h l)"),
                               start=True, stop=True).then_inc(diff_done, 1)
                        token_unit(U_SSD, u + 8, i, N_SSD, h_hi, h_lo, 8, DC - 1, zout)
                        token_unit(U_SSD, u + 9, i, N_SSD, h_hi, h_lo, 12, DC - 1, zout)
                        pe.wait_ge(xdt_ready, grp + 1)
                        pe.wait_ge(mt_ready, grp * 4 + 4)
                        for b in range(BLK):
                            for h in range(HG):
                                mm(aux[:, b, h * HD:h * HD + HD], mt[:, b, h, :], xdt[:, b, h * HD:h * HD + HD],
                                   start=True, stop=True)
                        mm(aux[:, 3, :], cbm[:, 2, :], xend[:, :], start=True, stop=True).then_inc(y_done, 1)
            if on("g0"):
                with pe.Fori(0, 2) as i:
                    for s in range(2):
                        for q in range(4):
                            channel_unit(U_G0, 4 * s + q, i, N_G0, h_hi, h_lo, 4 * q, DC - 1, slab_tiles(1 - s))
            if on("yt"):
                pe.wait_ge(ytok_ready, GROUPS)
                for g in range(GROUPS):
                    if g >= 2:
                        pe.wait_ge(yt_split, g - 1)
                    for t in range(4):
                        for b in range(BLK):
                            last = nc.tensor.transpose(
                                aux[:, 2 * (g % 2) + t // 2, (t % 2) * SEQ + b * P:(t % 2) * SEQ + b * P + P],
                                y_tok[:, b, g * W + t * P:g * W + t * P + P], ident)
                    last.then_inc(yt_turned, 1)
            if on("so"):
                pe.wait_ge(yt_split, GROUPS)
                with pe.Fori(0, 2) as i:
                    for s in range(2):
                        for q in range(8):
                            channel_unit(U_SO, 8 * s + q, i, N_SO, yT_hi, yT_lo, 4 * q, 2 * DC - 1, slab_tiles(1 - s))
            if on("ada2"):
                with pe.Fori(0, 8) as i:
                    for j in range(2):
                        ada_slab(U_ADA2, i, j, 1 - j)
                        pe.wait_ge(adarow_ready, i * 2 + (8 + j + 3))
                        mm(aux[:, j, :], con[0:2, C_ONE:C_ONE + P], adarow[:, j, :], start=True, stop=True)\
                            .then_inc(bc_turned, 1)
            if on("mix"):
                pe.wait_ge(mx_split, 4)
                with pe.Fori(0, 2) as i:
                    for s in range(2):
                        for q in range(4):
                            token_unit(U_MIX, 4 * s + q, i, N_MIX, mx_hi, mx_lo, 4 * q, DC - 1,
                                       [ps[:, 1 - s, b, :] for b in range(BLK)])
            if on("h2"):
                for b in range(BLK):
                    pe.wait_ge(h2_ready, b + 1)
                    for t in range(DC):
                        last = nc.tensor.transpose((auxf, psf)[b][:, t * P:t * P + P], h2[:, b, t * P:t * P + P], ident)
                    last.then_inc(h2_turned, 1)
            if on("wq"):
                pe.wait_ge(h2_split, BLK)
                for s in range(4):
                    for q in range(4):
                        channel_unit(U_WQ, 4 * s + q, 0, 0, h2_hi, h2_lo, 4 * q, DC - 1, slab_tiles(1 - s % 2))
                pe.wait_ge(qT_a, 4)
                pe.wait_ge(qT_v, 4)
                for b in range(BLK):
                    for t in range(2 * PEER_HEADS):
                        last = mm((auxf, psf)[b][:, t * KEYS:t * KEYS + KEYS], qT[:, t, b * P:b * P + P],
                                  keysT[:, t % 2, :], start=True, stop=True)
                    last.then_inc(score_done, 1)

        @block.scalar
        def _(act):
            F = nc.scalar.activation
            S = Steps(act, act_step)

            def hi(base, j, i, per, cols_=W):
                n = base + j
                act.wait_ge(raw_full[n % 4], full_count(base, j, i, per))
                act.wait_ge(pe_used, i * per + (n + 1))
                F(whi[:, n % 2, :, 0:cols_], raw[:, n % 4, :, 0:cols_], ACT.Copy).then_inc(hi_ready, 1)

            def hi_flat(base, j, i, per, count):
                n = base + j
                act.wait_ge(raw_full[n % 4], full_count(base, j, i, per))
                act.wait_ge(pe_used, i * per + (n + 1))
                F(whi[:, n % 2].rearrange("p a b -> p (a b)")[:, 0:count],
                  raw[:, n % 4].rearrange("p a b -> p (a b)")[:, 0:count], ACT.Copy).then_inc(hi_ready, 1)

            def slab_done(base, j, i, per):
                act.wait_ge(pe_used, i * per + (base + j + 3))

            def root(dst, src, scale):
                F(dst, src, ACT.Sqrt, bias=con[:, C_EPS:C_EPS + 1], scale=scale).then_inc(std_ready, 1)

            def norm_root(number):
                act.wait_ge(var_ready, number)
                root(st[:, 46:47], st[:, 45:46], 1.0)

            act.wait_ge(cols_ready, 1)
            F(csil[:, :], cols[:, PC_C:PC_C + DC], ACT.Silu).then_inc(c_hi_ready, 1)
            act.wait_ge(c_hi_ready, 1)
            F(cs2[:, :, 0], csil[:, :], ACT.Copy).then_inc(c_hi_ready, 1)
            act.wait_ge(params_in, 16 * 17)
            F(anegA[:, :], anegA[:, :], ACT.Exp).then_inc(neg_a, 1)
            for b in range(BLK):
                norm_root(b + 1)
            for r in range(4):
                act.wait_ge(x_turned, r + 1)
                F(xnT[:, 4 * r:4 * r + 4, :].rearrange("p k t -> p (k t)"),
                  auxf[:, 1024 * (r % 2):1024 * (r % 2) + 1024], ACT.Copy).then_inc(xT_ready, 1)
            hi(U_ADA1, 0, 0, 0)
            act.wait_ge(angles_ready, 1)
            for k, tab_ in enumerate((sin2, cos2)):
                for e in range(2):
                    last = F(tab_[:, :, 32 * e:32 * e + 32], angs[:, k], ACT.Sin)
                    last.then_inc(sines_ready, 1)
            with act.Fori(0, 4) as i:
                for u in range(8):
                    hi(U_ADA1, u + 1, i, 8)
            for q in range(4):
                act.wait_ge(h_full, q + 1)
                F(h_hi[:, 4 * q:4 * q + 4, :], xnT[:, 4 * q:4 * q + 4, :], ACT.Copy).then_inc(h_hi_ready, 1)
            if on("low"):
                def sumsq(s):
                    for b in range(BLK):
                        if s or b:
                            act.wait_ge(sumsq_ready, 2 * s + b)
                        F(junk[:, :], ps[:, s, b, :], ACT.Square, accum_out=st[:, 32 + 2 * s + b:33 + 2 * s + b])\
                            .then_inc(sumsq_ready, 1)
                    act.wait_ge(sumsq_ready, 2 * s + 2)
                    root(st[:, 36 + 2 * s:38 + 2 * s], st[:, 32 + 2 * s:34 + 2 * s], 1.0 / RANK)

                def split_cn(s, norm_col, dst):
                    act.wait_ge(cn_turned, s + 1)
                    for t in range(RC):
                        F(dst[:, t, :], auxf[:, 1024 * s + t * SEQ:1024 * s + (t + 1) * SEQ], ACT.Copy,
                          scale=cols[:, norm_col + t:norm_col + t + 1]).then_inc(cn_hi_ready, 1)

                for u in (1, 2, 3, 4):
                    hi(U_LOW, u, 0, 0)
                slab_done(U_LOW, 3, 0, 0)
                sumsq(0)
                for u in (5, 6, 7):
                    hi(U_LOW, u, 0, 0)
                hi_flat(U_LOW, 8, 0, 0, DC * 64)
                slab_done(U_LOW, 7, 0, 0)
                sumsq(1)
                split_cn(0, PC_QN, cqT_hi)
                hi_flat(U_LOW, 9, 0, 0, DC * 64)
                hi(U_ATT, 0, 0, 0)
                act.wait_ge(sp_x, 1)
                F(sp[3][:, :, :], sp[2][:, :, :], ACT.Exp).then_inc(sp_e, 1)
                split_cn(1, PC_KVN, ckT_hi)
                act.wait_ge(cum_ready, 1)
                F(toend[:, :], aux[:, 0, 0:HEADS], ACT.Exp)
                F(fromst[:, :], aux[:, 0, HEADS:2 * HEADS], ACT.Exp).then_inc(decay_ready, 1)
                act.wait_ge(kpe_turned, 1)
                F(kpeT[:, :], aux[:, 1, 0:SEQ], ACT.Copy).then_inc(kpe_read, 1)
            if on("att"):
                with act.Fori(0, 4) as i:
                    hi(U_ATT, 1, i, N_ATT)
                    hi(U_ATT, 2, i, N_ATT)
                    slab_done(U_ATT, 1, i, N_ATT)
                    F(qr[:, :, :, :].rearrange("p b h n -> p (b h n)"), ps[:, 0, 0, :], ACT.Copy).then_inc(qr_copied, 1)
                    F(qn[:, 0:2, :].rearrange("p h t -> p (h t)"), ps[:, 1, 0, :], ACT.Copy)
                    hi(U_ATT, 3, i, N_ATT)
                    hi(U_ATT, 4, i, N_ATT)
                    slab_done(U_ATT, 3, i, N_ATT)
                    F(kn[:, 0:2, :].rearrange("p h t -> p (h t)"), aux[:, 2, :], ACT.Copy)
                    F(vt[:, 0, :], aux[:, 0, :], ACT.Copy).then_inc(att_evac_a, 1)
                    hi(U_ATT, 5, i, N_ATT)
                    act.wait_ge(qpe_turned, i + 1)
                    F(qpeT[:, :, :].rearrange("p h t -> p (h t)"), aux[:, 2, :], ACT.Copy).then_inc(qpe_read, 1)
                    hi(U_ATT, 6, i, N_ATT)
                    hi(U_ATT, 7, i, N_ATT)
                    act.wait_ge(negmax_ready, i + 1)
                    for h in range(4):
                        for b in range(BLK):
                            c = slice(b * P, P + b * 2 * P)
                            last = F(probs[:, h, c], aux[:, h, c], ACT.Exp, bias=st[:, 8 + 4 * b + h:9 + 4 * b + h],
                                     scale=SCALE, accum_out=st[:, 16 + 4 * b + h:17 + 4 * b + h])
                    last.then_inc(exp_done, 1)
                    hi(U_ATT, 8, i, N_ATT)
                    for h in (0, 2):
                        act.wait_ge(probs_turned, i * 4 + (h + 1))
                        F(pT[:, h, :], aux[:, h, 0:3 * P], ACT.Copy).then_inc(pT_a, 1)
                    act.wait_ge(pv_done, i + 1)
                    F(oT[:, ds(i * 4, 4), :], aux[:, :, 0:SEQ], ACT.Copy).then_inc(o_read, 1)
                    for t in range(4):
                        last = F(premix[:, ds(i * 4 + t, 1), :].rearrange("p a t -> p (a t)"),
                                 ps[:, 0, t // 2, (t % 2) * SEQ:(t % 2) * SEQ + SEQ], ACT.Sigmoid,
                                 bias=cols[:, ds(i * 4 + (PC_BG + DC + t), 1)])
                    last.then_inc(b_free, 1)
            if on("mla"):
                act.wait_ge(o_read, 4)
                for q in range(4):
                    F(oT_hi[:, 4 * q:4 * q + 4, :], oT[:, 4 * q:4 * q + 4, :], ACT.Copy).then_inc(o_hi_ready, 1)
                with act.Fori(0, 2) as i:
                    for u in range(8):
                        hi(U_MLA, u + 1, i, N_MLA)
            if on("ssd"):
                with act.Fori(0, 4) as i:
                    for g in range(2):
                        u = 10 * g
                        grp = i * 2 + g
                        for k in (1, 2, 3, 4, 5):
                            hi(U_SSD, u + k, i, N_SSD)
                        for t in range(4):
                            if t == 2:
                                hi(U_SSD, u + 6, i, N_SSD)
                            act.wait_ge(conv_done, grp * 6 + (t + 1))
                            F(xc[:, t, :], xc[:, t, :], ACT.Silu).then_inc(silu_done, 1)
                        hi(U_SSD, u + 7, i, N_SSD)
                        act.wait_ge(conv_done, grp * 6 + 6)
                        F(bcT[:, :, :], bcT[:, :, :], ACT.Silu).then_inc(silu_done, 1)
                        hi(U_SSD, u + 8, i, N_SSD)
                        act.wait_ge(xt_turned, grp + 1)
                        F(x_tok[:, :, :].rearrange("p b n -> p (b n)"), auxf[:, 0:1024], ACT.Copy).then_inc(xt_ready, 1)
                        hi(U_SSD, u + 9, i, N_SSD)
                        for k in range(4):
                            act.wait_ge(diff_done, grp * 4 + (k + 3))
                            F(mt[:, k // 2, 4 * (k % 2):4 * (k % 2) + 4, :].rearrange("p h l -> p (h l)"),
                              aux[:, 3 - k % 2, :], ACT.Exp).then_inc(decay_exp, 1)
                        hi(U_SSD, u + 10, i, N_SSD)
                        slab_done(U_SSD, u + 9, i, N_SSD)
                        F(zs[:, :, :], ps[:, 1 - g, :, :], ACT.Silu).then_inc(z_silu, 1)
                        act.wait_ge(yg_ready, grp + 1)
                        for b in range(BLK):
                            if b:
                                act.wait_ge(ysq_ready, grp * 2 + 1)
                            last = F(yjunk[:, :], yg[:, b, :], ACT.Square, accum_out=st[:, 40 + b:41 + b])
                            last.then_inc(ysq_ready, 1)
                        act.wait_ge(ysq_ready, grp * 2 + 2)
                        root(st[:, 42:44], st[:, 40:42], 1.0 / W)
            if on("g0"):
                with act.Fori(0, 2) as i:
                    for s in range(2):
                        for q in range(4):
                            hi(U_G0, 4 * s + q + 1, i, N_G0)
                        slab_done(U_G0, 4 * s + 3, i, N_G0)
                        for t in range(4):
                            last = F(g0[:, ds(i * 8 + (4 * s + t), 1), :].rearrange("p a t -> p (a t)"),
                                     ps[:, 1 - s, t // 2, (t % 2) * SEQ:(t % 2) * SEQ + SEQ], ACT.Sigmoid,
                                     bias=cols[:, ds(i * 8 + (PC_BG + 4 * s + t), 1)])
                        last.then_inc(g0_ready, 1)
            if on("yt"):
                for g in range(GROUPS):
                    act.wait_ge(yt_turned, g + 1)
                    for t in range(4):
                        F(yT_hi[:, 4 * g + t, :], auxf[:, 1024 * (g % 2) + t * SEQ:1024 * (g % 2) + (t + 1) * SEQ],
                          ACT.Copy, scale=cols[:, PC_NW + 4 * g + t:PC_NW + 4 * g + t + 1]).then_inc(yt_hi, 1)
            if on("so"):
                with act.Fori(0, 2) as i:
                    for u in range(16):
                        hi(U_SO, u + 1, i, N_SO)
            if on("ada2"):
                act.wait_ge(premix_ready, 8)
                for q in range(4):
                    F(mx_hi[:, 4 * q:4 * q + 4, :], premix[:, 4 * q:4 * q + 4, :], ACT.Copy).then_inc(mx_hi_ready, 1)
                bc = adabc[:, :, :].rearrange("p v n -> p (v n)")
                with act.Fori(0, 8) as i:
                    for j in range(2):
                        for q in range(4):
                            hi(U_ADA2, 4 * j + q + 1, i, 8)
                        act.wait_ge(bc_turned, i * 2 + (j + 1))
                        F(bc[:, ds(i * 2 * W + j * W, W)], aux[:, j, :], ACT.Copy).then_inc(bc_read, 1)
            if on("mix"):
                with act.Fori(0, 2) as i:
                    for u in range(8):
                        hi(U_MIX, u + 1, i, N_MIX)
            if on("h2"):
                for n in range(2 * BLK):
                    norm_root(n + 3)
                for b in range(BLK):
                    act.wait_ge(h2_turned, b + 1)
                    F(h2_hi[:, :, b * P:b * P + P], (auxf, psf)[b].rearrange("p (k t) -> p k t", t=P), ACT.Copy)\
                        .then_inc(h2_hi_ready, 1)
            if on("wq"):
                for s in range(4):
                    for q in range(4):
                        if U_WQ + 4 * s + q + 1 < U_END:
                            hi(U_WQ, 4 * s + q + 1, 0, 0)
                    slab_done(U_WQ, 4 * s + 3, 0, 0)
                    F(qT[:, 4 * s:4 * s + 2, :].rearrange("p k t -> p (k t)"), ps[:, 1 - s % 2, 0, :], ACT.Copy)\
                        .then_inc(qT_a, 1)
                act.wait_ge(score_done, 1)
                F(score[:, 0:PEER_HEADS, :].rearrange("p h k -> p (h k)"), auxf, ACT.Copy).then_inc(score_a, 1)
            if on("all"):
                for b in range(BLK):
                    if b:
                        act.wait_ge(row_used, ROWS + 2 * TOPK * PEER_HEADS * b)
                    else:
                        act.wait_ge(score_a, 1)
                    F(auxf, h2[:, b, :], ACT.Copy).then_inc(h2_psum, 1)

                    def gate(n_expr, k):
                        act.wait_ge(top_ready, n_expr)
                        F(gex[:, k, :], tval[:, k, :], ACT.Exp, bias=ngm[:, k:k + 1], accum_out=gsum[:, k:k + 1])\
                            .then_inc(gate_exp, 1)

                    if b == 0:
                        gate(1, 0)

                    def pair(i, last_one):
                        for k in range(2):
                            act.wait_ge(row_used, i * (4 * TOPK) + (ROWS + (PEER_HEADS * b + k) * 2 * TOPK + TOPK))
                            F(gel[:, k, :], dots[:, k, :], ACT.Gelu).then_inc(gelu_ready, 1)
                            if not (last_one and k == 1):
                                gate(i * 2 + (PEER_HEADS * b + k + 2), 1 - k)

                    with act.Fori(0, 4 - b) as i:
                        pair(i, False)
                    if b:
                        pair(3, True)
                    norm_root(b + 7)

        @block.vector
        def _(dve):
            V = nc.vector
            S = Steps(dve, dve_step)
            link = S.link

            def lo(base, j, i, per, cols_=W):
                n = base + j
                dve.wait_ge(hi_ready, i * per + (n + 1))
                V.tensor_tensor(wlo[:, n % 2, :, 0:cols_], raw[:, n % 4, :, 0:cols_],
                                whi[:, n % 2, :, 0:cols_].bitcast(F32), ALU.subtract).then_inc(lo_ready, 1)

            def lo_flat(base, j, i, per, count):
                n = base + j
                dve.wait_ge(hi_ready, i * per + (n + 1))
                flat = lambda w: w.rearrange("p a b -> p (a b)")[:, 0:count]
                V.tensor_tensor(flat(wlo[:, n % 2]), flat(raw[:, n % 4]), flat(whi[:, n % 2]).bitcast(F32),
                                ALU.subtract).then_inc(lo_ready, 1)

            def slab_done(base, j, i, per):
                dve.wait_ge(pe_used, i * per + (base + j + 3))

            def rsqrt(cols_, number):
                dve.wait_ge(std_ready, number)
                link(V.reciprocal(cols_, cols_))

            def normalise(dst, src, number):
                for k in range(4):
                    S.step(V.bn_stats(bn[:, k, :], src[:, k * W:(k + 1) * W]))
                S.wait()
                V.bn_aggr(st[:, 44:46], bn[:, :, :].rearrange("p a b -> p (a b)")).then_inc(var_ready, 1)
                rsqrt(st[:, 46:47], number)
                return V.tensor_scalar(dst, src, st[:, 44:45], st[:, 46:47], ALU.subtract, ALU.mult)

            dve.sem_inc(lo_ready, 4)
            dve.sem_inc(adarow_ready, 2)
            dve.sem_inc(row_used, ROWS)
            dve.wait_ge(rows_turned, 1)
            V.tensor_copy(cols[:, :], aux[:, 0, 0:COLS_ALL]).then_inc(cols_ready, 1)
            dve.wait_ge(rows_turned, 2)
            V.tensor_copy(keysT[:, :, :].rearrange("p a b -> p (a b)"), aux[:, 1, 0:2 * KEYS]).then_inc(cols_ready, 1)
            dve.wait_ge(c_hi_ready, 2)
            V.tensor_tensor(cs2[:, :, 1], csil[:, :], cs2[:, :, 0].bitcast(F32), ALU.subtract).then_inc(c_ready, 1)
            dve.wait_ge(x_loaded, 16 * BLK)
            for b in range(BLK):
                normalise(x_in[:, b, :], x_in[:, b, :], b + 1).then_inc(x_normed, 1)
            lo(U_ADA1, 0, 0, 0)
            link(V.tensor_copy(posf[:, :], posi[:, :]))
            for b in range(BLK):
                S.step(V.tensor_scalar(ang[:, b, :], con[:, C_FREQ:C_FREQ + 32], posf[:, b:b + 1], None, ALU.mult))
            S.wait()
            c1 = 6.28125
            c2 = float(np.float32(np.round((2 * math.pi - c1) * 2 ** 21) / 2 ** 21))
            c3 = float(np.float32(2 * math.pi - c1 - c2))
            for k in range(2):
                link(V.tensor_scalar(turn[:, :, :], ang[:, :, :], 1 / (2 * math.pi), 0.25 * k, ALU.mult, ALU.add))
                link(V.tensor_scalar(turn[:, :, :], turn[:, :, :], 12582912.0, None, ALU.add))
                link(V.tensor_scalar(turn[:, :, :], turn[:, :, :], 12582912.0, None, ALU.subtract))
                src = ang
                for c in (c1, c2, c3):
                    link(V.scalar_tensor_tensor(angs[:, k], turn[:, :, :], -c, src[:, :, :] if src is ang else src,
                                                ALU.mult, ALU.add))
                    src = angs[:, k]
                link(V.tensor_scalar(angs[:, k], angs[:, k], k * math.pi / 2, 3.1415925, ALU.add, ALU.min))
                last = V.tensor_scalar(angs[:, k], angs[:, k], -3.1415925, None, ALU.max)
                S.step(last) if k == 0 else last.then_inc(angles_ready, 1)

            with dve.Fori(0, 4) as i:
                S.enter(i, 2)
                for j in range(2):
                    for q in range(4):
                        lo(U_ADA1, 4 * j + q + 1, i, 8)
                    slab_done(U_ADA1, 4 * j + 3, i, 8)
                    dve.wait_ge(bias_in[j], i * 16 + 16)
                    V.tensor_tensor(adarow[:, j, :], ps[0:2, j, 0, :], bias2[:, j, :], ALU.add)\
                        .then_inc(adarow_ready, 1)
                    dve.wait_ge(ada_turned, i * 2 + (j + 1))
                    S.step(V.tensor_copy(adacol[:, ds(i * 8 + 4 * j, 4)], aux[:, 3, 4 * j:4 * j + 4]))
            S.leave(4)
            S.wait()
            link(V.tensor_scalar(adacol[:, DC:2 * DC], adacol[:, DC:2 * DC], 1.0, None, ALU.add))
            for q in range(4):
                for k in range(4 * q, 4 * q + 4):
                    last = V.tensor_scalar(xnT[:, k, :], xnT[:, k, :], adacol[:, DC + k:DC + k + 1],
                                           adacol[:, k:k + 1], ALU.mult, ALU.add)
                    S.step(last) if k % 4 < 3 else last.then_inc(h_full, 1)
            for q in range(4):
                dve.wait_ge(h_hi_ready, q + 1)
                V.tensor_tensor(h_lo[:, 4 * q:4 * q + 4, :], xnT[:, 4 * q:4 * q + 4, :],
                                h_hi[:, 4 * q:4 * q + 4, :].bitcast(F32), ALU.subtract).then_inc(h_ready, 1)
            if on("low"):
                def rms(s):
                    rsqrt(st[:, 36 + 2 * s:38 + 2 * s], s + 3)
                    if s:
                        dve.wait_ge(cn_turned, s)
                    for b in range(BLK):
                        last = V.tensor_scalar(cn[:, b, :], ps[:, s, b, :], st[:, 36 + 2 * s + b:37 + 2 * s + b],
                                               None, ALU.mult)
                        S.step(last) if b == 0 else last.then_inc(cn_ready, 1)

                def split_cn(s, norm_col, dst_hi, dst_lo):
                    for t in range(RC):
                        dve.wait_ge(cn_hi_ready, RC * s + (t | 1) + 1)
                        last = V.scalar_tensor_tensor(
                            dst_lo[:, t, :], auxf[:, 1024 * s + t * SEQ:1024 * s + (t + 1) * SEQ],
                            cols[:, norm_col + t:norm_col + t + 1], dst_hi[:, t, :].bitcast(F32),
                            ALU.mult, ALU.subtract)
                        S.step(last) if t < RC - 1 else last.then_inc(cn_split, 1)

                for u in (1, 2, 3, 4):
                    lo(U_LOW, u, 0, 0)
                slab_done(U_LOW, 3, 0, 0)
                rms(0)
                for u in (5, 6, 7):
                    lo(U_LOW, u, 0, 0)
                lo_flat(U_LOW, 8, 0, 0, DC * 64)
                slab_done(U_LOW, 7, 0, 0)
                rms(1)
                split_cn(0, PC_QN, cqT_hi, cqT_lo)
                lo_flat(U_LOW, 9, 0, 0, DC * 64)
                lo(U_ATT, 0, 0, 0)
                slab_done(U_LOW, 9, 0, 0)
                bc = dtb[:, :].unsqueeze(1).broadcast_to([P, BLK, HEADS])
                link(V.tensor_tensor(sp[0][:, :, :], ps[:, 0, :, 0:HEADS], bc, ALU.add))
                link(V.tensor_scalar(sp[1][:, :, :], sp[0][:, :, :], -1.0, None, ALU.mult))
                V.tensor_tensor(sp[2][:, :, :], sp[0][:, :, :], sp[1][:, :, :], ALU.min).then_inc(sp_x, 1)
                dve.wait_ge(sines_ready, 4)
                S.step(V.tensor_tensor(krt[:, :, :], ps[:, 0, :, 64:128], cos2[:, :, :], ALU.mult))
                V.tensor_tensor(krs[:, :, :], ps[:, 0, :, 64:128], sin2[:, :, :], ALU.mult).then_inc(b_free, 1)
                dve.wait_ge(b_free, 1)
                S.wait()
                for e in range(2):
                    S.step(V.tensor_tensor(kpe2[:, :, e, 0:32], krt[:, :, 0:32], krs[:, :, 32:64], ALU.subtract))
                    last = V.tensor_tensor(kpe2[:, :, e, 32:64], krs[:, :, 0:32], krt[:, :, 32:64], ALU.add)
                    S.step(last) if e == 0 else last.then_inc(kpe_ready, 1)
                dve.wait_ge(sp_e, 1)
                s0, s1, s2, s3, s4, s5 = (t[:, :, :] for t in sp)
                link(V.tensor_scalar(s4, s3, 2.0, None, ALU.add))
                link(V.reciprocal(s5, s4))
                link(V.tensor_tensor(s4, s3, s5, ALU.mult))
                link(V.tensor_tensor(s5, s4, s4, ALU.mult))
                link(V.tensor_scalar(s1, s5, 1 / 17, None, ALU.mult))
                for k in (15, 13, 11, 9, 7, 5, 3):
                    link(V.scalar_tensor_tensor(s1, s1, 1 / k, s5, ALU.add, ALU.mult))
                link(V.scalar_tensor_tensor(s1, s1, 1.0, s4, ALU.add, ALU.mult))
                link(V.tensor_scalar(s2, s0, 0.0, None, ALU.max))
                link(V.scalar_tensor_tensor(dtv[:, :, :], s1, 2.0, s2, ALU.mult, ALU.add))
                dve.wait_ge(neg_a, 1)
                V.scalar_tensor_tensor(adt[:, :, :], dtv[:, :, :], -1.0,
                                       anegA[:, :].unsqueeze(1).broadcast_to([P, BLK, HEADS]),
                                       ALU.mult, ALU.mult).then_inc(adt_ready, 1)
                split_cn(1, PC_KVN, ckT_hi, ckT_lo)
            if on("att"):
                cosb, sinb = (t[:, :, :].unsqueeze(2).broadcast_to([P, BLK, 4, ROPE]) for t in (cos2, sin2))
                with dve.Fori(0, 4) as i:
                    S.enter(i, 9)
                    lo(U_ATT, 1, i, N_ATT)
                    lo(U_ATT, 2, i, N_ATT)
                    slab_done(U_ATT, 1, i, N_ATT)
                    S.step(V.tensor_copy(qn[:, 2:4, :].rearrange("p h t -> p (h t)"), ps[:, 1, 1, :]))
                    dve.wait_ge(qr_copied, i + 1)
                    for b in range(BLK):
                        S.step(V.tensor_tensor(qrt[:, b], qr[:, b], cosb[:, b], ALU.mult))
                        S.step(V.tensor_tensor(qrs[:, b], qr[:, b], sinb[:, b], ALU.mult))
                    S.wait()
                    S.step(V.tensor_tensor(qr[:, :, :, 0:32], qrt[:, :, :, 0:32], qrs[:, :, :, 32:64], ALU.subtract))
                    V.tensor_tensor(qr[:, :, :, 32:64], qrs[:, :, :, 0:32], qrt[:, :, :, 32:64], ALU.add)\
                        .then_inc(qr_ready, 1)
                    lo(U_ATT, 3, i, N_ATT)
                    lo(U_ATT, 4, i, N_ATT)
                    slab_done(U_ATT, 3, i, N_ATT)
                    V.tensor_copy(kn[:, 2:4, :].rearrange("p h t -> p (h t)"), aux[:, 3, :])
                    V.tensor_copy(vt[:, 1, :], aux[:, 1, :]).then_inc(att_evac_v, 1)
                    lo(U_ATT, 5, i, N_ATT)
                    lo(U_ATT, 6, i, N_ATT)
                    lo(U_ATT, 7, i, N_ATT)
                    dve.wait_ge(scores_done, i + 1)
                    for b in range(BLK):
                        S.step(V.tensor_reduce(st[:, 4 * b:4 * b + 4], aux[:, :, b * P:P + b * 2 * P], AX_X, ALU.max))
                    S.wait()
                    V.tensor_scalar(st[:, 8:16], st[:, 0:8], -SCALE, None, ALU.mult).then_inc(negmax_ready, 1)
                    dve.wait_ge(exp_done, i + 1)
                    link(V.reciprocal(st[:, 24:32], st[:, 16:24]))
                    for b in range(BLK):
                        c = slice(b * P, P + b * 2 * P)
                        last = V.tensor_tensor(probs[:, :, c], probs[:, :, c],
                                               st[:, 24 + 4 * b:28 + 4 * b].unsqueeze(2).broadcast_to([P, 4, P * (b + 1)]),
                                               ALU.mult)
                        if b:
                            last.then_inc(probs_ready, 1)
                    lo(U_ATT, 8, i, N_ATT)
                    for h in (1, 3):
                        dve.wait_ge(probs_turned, i * 4 + (h + 1))
                        V.tensor_copy(pT[:, h, :], aux[:, h, 0:3 * P]).then_inc(pT_v, 1)
                S.leave(4)
            if on("mla"):
                for q in range(4):
                    dve.wait_ge(o_hi_ready, q + 1)
                    V.tensor_tensor(oT_lo[:, 4 * q:4 * q + 4, :], oT[:, 4 * q:4 * q + 4, :],
                                    oT_hi[:, 4 * q:4 * q + 4, :].bitcast(F32), ALU.subtract).then_inc(o_split, 1)
                dve.wait_ge(b_free, 5)
                with dve.Fori(0, 2) as i:
                    S.enter(i, 4)
                    for s in range(2):
                        for q in range(4):
                            lo(U_MLA, 4 * s + q + 1, i, N_MLA)
                        slab_done(U_MLA, 4 * s + 3, i, N_MLA)
                        for k in range(2):
                            m = premix[:, ds(i * 8 + (4 * s + 2 * k), 2), :]
                            S.step(V.tensor_tensor(m, ps[:, 1 - s, k, :].rearrange("p (k t) -> p k t", t=SEQ), m,
                                                   ALU.mult))
                S.leave(2)
            if on("ssd"):
                with dve.Fori(0, 4) as i:
                    S.enter(i, 2 * 25)
                    for g in range(2):
                        u = 10 * g
                        grp = i * 2 + g
                        for k in (1, 2, 3, 4, 5):
                            lo(U_SSD, u + k, i, N_SSD)

                        def conv(dst, src, tile):
                            w_ = [cols[:, ds(tile + c, 1)] for c in PC_CW]
                            link(V.tensor_scalar(dst, src, w_[3], cols[:, ds(tile + PC_CB, 1)], ALU.mult, ALU.add))
                            for j in (2, 1, 0):
                                s = 3 - j
                                last = V.scalar_tensor_tensor(dst[:, s:SEQ], src[:, 0:SEQ - s], w_[j], dst[:, s:SEQ],
                                                              ALU.mult, ALU.add)
                                link(last) if j else last.then_inc(conv_done, 1)

                        slab_done(U_SSD, u + 3, i, N_SSD)
                        for t in range(4):
                            conv(xc[:, t, :], ps[:, 1 - g, t // 2, (t % 2) * SEQ:(t % 2) * SEQ + SEQ], i * 8 + (4 * g + t))
                        lo(U_SSD, u + 6, i, N_SSD)
                        slab_done(U_SSD, u + 4, i, N_SSD)
                        conv(bcT[:, 0, :], ps[:, g, 0, 0:SEQ], i * 2 + (32 + g))
                        lo(U_SSD, u + 7, i, N_SSD)
                        slab_done(U_SSD, u + 5, i, N_SSD)
                        conv(bcT[:, 1, :], ps[:, g, 1, 0:SEQ], i * 2 + (40 + g))
                        lo(U_SSD, u + 8, i, N_SSD)
                        lo(U_SSD, u + 9, i, N_SSD)
                        dve.wait_ge(cb_done, grp + 1)
                        S.step(V.tensor_tensor(cbm[:, 0:2, :], aux[:, 2, 0:2 * P].rearrange("p (k l) -> p k l", l=P),
                                               upper.unsqueeze(1).broadcast_to([P, 2, P]), ALU.mult))
                        V.tensor_copy(cbm[:, 2, :], aux[:, 2, 2 * P:3 * P]).then_inc(cb_read, 1)
                        S.wait()
                        for k in range(4):
                            dve.wait_ge(decay_exp, grp * 4 + (k + 1))
                            m = mt[:, k // 2, 4 * (k % 2):4 * (k % 2) + 4, :]
                            V.tensor_tensor(m, m, cbm[:, k // 2, :].unsqueeze(1).broadcast_to([P, 4, P]), ALU.mult)\
                                .then_inc(mt_ready, 1)
                        lo(U_SSD, u + 10, i, N_SSD)
                        dve.wait_ge(y_done, grp + 1)
                        dve.wait_ge(xskip_ready, grp + 1)
                        y1 = yg[:, 1, :]
                        link(V.tensor_tensor(y1.rearrange("p (h d) -> p h d", d=HD),
                                             aux[:, 3, :].rearrange("p (h d) -> p h d", d=HD),
                                             fromst[:, ds(i * 2 * HG + g * HG, HG)].unsqueeze(2).broadcast_to([P, HG, HD]),
                                             ALU.mult))
                        link(V.tensor_tensor(y1, y1, aux[:, 1, :], ALU.add))
                        S.step(V.tensor_tensor(y1, y1, x_tok[:, 1, :], ALU.add))
                        S.step(V.tensor_tensor(yg[:, 0, :], aux[:, 0, :], x_tok[:, 0, :], ALU.add))
                        S.wait()
                        dve.wait_ge(z_silu, grp + 1)
                        V.tensor_tensor(yg[:, :, :], yg[:, :, :], zs[:, :, :], ALU.mult).then_inc(yg_ready, 1)
                        rsqrt(st[:, 42:44], grp + 5)
                        for b in range(BLK):
                            last = V.tensor_scalar(y_tok[:, b, ds(i * 2 * W + g * W, W)], yg[:, b, :],
                                                   st[:, 42 + b:43 + b], None, ALU.mult)
                            S.step(last) if b == 0 else last.then_inc(ytok_ready, 1)
                            if b == 0:
                                S.wait()
                S.leave(4)
            if on("g0"):
                with dve.Fori(0, 2) as i:
                    for u in range(8):
                        lo(U_G0, u + 1, i, N_G0)
            if on("yt"):
                for g in range(GROUPS):
                    for t in range(4):
                        dve.wait_ge(yt_hi, 4 * g + (t | 1) + 1)
                        last = V.scalar_tensor_tensor(
                            yT_lo[:, 4 * g + t, :], auxf[:, 1024 * (g % 2) + t * SEQ:1024 * (g % 2) + (t + 1) * SEQ],
                            cols[:, PC_NW + 4 * g + t:PC_NW + 4 * g + t + 1], yT_hi[:, 4 * g + t, :].bitcast(F32),
                            ALU.mult, ALU.subtract)
                        S.step(last) if t < 3 else last.then_inc(yt_split, 1)
            if on("so"):
                dve.wait_ge(g0_ready, 4)
                with dve.Fori(0, 2) as i:
                    S.enter(i, 4)
                    for s in range(2):
                        for q in range(8):
                            lo(U_SO, 8 * s + q + 1, i, N_SO)
                        slab_done(U_SO, 8 * s + 7, i, N_SO)
                        for k in range(2):
                            m = ds(i * 8 + (4 * s + 2 * k), 2)
                            gt = gtmp[:, :].rearrange("p (k t) -> p k t", t=SEQ)
                            link(V.tensor_tensor(gt, ps[:, 1 - s, k, :].rearrange("p (k t) -> p k t", t=SEQ),
                                                 g0[:, m, :], ALU.mult))
                            V.tensor_tensor(premix[:, m, :], premix[:, m, :], gt, ALU.add).then_inc(premix_ready, 1)
                            dve.wait_ge(premix_ready, i * 4 + (2 * s + k + 1))
                S.leave(2)
            if on("ada2"):
                for q in range(4):
                    dve.wait_ge(mx_hi_ready, q + 1)
                    V.tensor_tensor(mx_lo[:, 4 * q:4 * q + 4, :], premix[:, 4 * q:4 * q + 4, :],
                                    mx_hi[:, 4 * q:4 * q + 4, :].bitcast(F32), ALU.subtract).then_inc(mx_split, 1)
                with dve.Fori(0, 8) as i:
                    for j in range(2):
                        for q in range(4):
                            lo(U_ADA2, 4 * j + q + 1, i, 8)
                        slab_done(U_ADA2, 4 * j + 3, i, 8)
                        dve.wait_ge(bias_in[j], i * 16 + 16 * 5)
                        V.tensor_tensor(adarow[:, j, :], ps[0:2, 1 - j, 0, :], bias2[:, j, :], ALU.add)\
                            .then_inc(adarow_ready, 1)
            if on("mix"):
                dve.wait_ge(res_in, 16 * 4)
                dve.wait_ge(bc_read, 16)
                with dve.Fori(0, 2) as i:
                    S.enter(i, 8)
                    for s in range(2):
                        for q in range(4):
                            lo(U_MIX, 4 * s + q + 1, i, N_MIX)
                        slab_done(U_MIX, 4 * s + 3, i, N_MIX)
                        c = ds(i * 2 * W + s * W, W)
                        for b in range(BLK):
                            link(V.scalar_tensor_tensor(mtmp[:, :], gate1[:, c], 1.0, ps[:, 1 - s, b, :],
                                                        ALU.add, ALU.mult))
                            link(V.scalar_tensor_tensor(x1[:, b, c], x1[:, b, c], ALPHA, mtmp[:, :],
                                                        ALU.mult, ALU.add))
                S.leave(2)
            if on("h2"):
                for b in range(BLK):
                    link(normalise(x1[:, b, :], x1[:, b, :], 2 * b + 13))
                    link(V.tensor_tensor(x1[:, b, :], x1[:, b, :], ln1[:, 0, :], ALU.mult))
                    link(V.tensor_tensor(x1[:, b, :], x1[:, b, :], ln1[:, 1, :], ALU.add))
                    link(normalise(h2[:, b, :], x1[:, b, :], 2 * b + 14))
                    link(V.scalar_tensor_tensor(h2[:, b, :], scale2, 1.0, h2[:, b, :], ALU.add, ALU.mult))
                    V.tensor_tensor(h2[:, b, :], h2[:, b, :], shift2, ALU.add).then_inc(h2_ready, 1)
                for b in range(BLK):
                    dve.wait_ge(h2_hi_ready, b + 1)
                    V.tensor_tensor(h2_lo[:, :, b * P:b * P + P], (auxf, psf)[b].rearrange("p (k t) -> p k t", t=P),
                                    h2_hi[:, :, b * P:b * P + P].bitcast(F32), ALU.subtract).then_inc(h2_split, 1)
            if on("wq"):
                for s in range(4):
                    for q in range(4):
                        if U_WQ + 4 * s + q + 1 < U_END:
                            lo(U_WQ, 4 * s + q + 1, 0, 0)
                    slab_done(U_WQ, 4 * s + 3, 0, 0)
                    V.tensor_copy(qT[:, 4 * s + 2:4 * s + 4, :].rearrange("p k t -> p (k t)"), ps[:, 1 - s % 2, 1, :])\
                        .then_inc(qT_v, 1)
                dve.wait_ge(score_done, 2)
                V.tensor_copy(score[:, PEER_HEADS:2 * PEER_HEADS, :].rearrange("p h k -> p (h k)"), psf)\
                    .then_inc(score_v, 1)
            if on("all"):
                NEG = -3.0e38
                iota = con[:, C_IOTA:C_IOTA + TOPK]

                def top16(vals, idx, src, work):
                    dve.sem_inc(held, 1)
                    link(V.max(vals[:, 0:8], src))
                    dve.sem_inc(held, 1)
                    link(V.max_index(idx[:, 0:8], vals[:, 0:8], src))
                    dve.sem_inc(held, 1)
                    link(V.match_replace(work, vals[:, 0:8], src, NEG))
                    dve.sem_inc(held, 1)
                    link(V.max(vals[:, 8:16], work))
                    dve.sem_inc(held, 1)
                    link(V.max_index(idx[:, 8:16], vals[:, 8:16], work))

                TOP_STEPS = 32

                def top(head, n_expr, k):
                    n0 = S.n
                    link(V.tensor_copy(scur[:, :, :].rearrange("p a b -> p (a b)"),
                                       score[:, ds(head, 1), :].rearrange("p a b -> p (a b)")))
                    for s in range(2):
                        top16(sval[:, s, :], sidx[:, s, :], scur[:, s, :], swork[:, s, :])
                    link(V.tensor_copy(sidf[:, :, :], sidx[:, :, :]))
                    link(V.tensor_tensor(cand[:, :, :], sval[:, 0, :].unsqueeze(2).broadcast_to([P, TOPK, TOPK]),
                                         sval[:, 1, :].unsqueeze(1).broadcast_to([P, TOPK, TOPK]), ALU.add))
                    top16(tval[:, k, :], tpos, cand[:, :, :].rearrange("p a b -> p (a b)"), cwork[:, :])
                    S.step(V.tensor_scalar(tab[:, 0, :], tpos[:, :], 4, None, ALU.logical_shift_right))
                    link(V.tensor_scalar(tab[:, 1, :], tpos[:, :], 15, None, ALU.bitwise_and))
                    link(V.tensor_copy(tabf[:, :, :], tab[:, :, :]))
                    for s in range(2):
                        link(V.tensor_tensor(onehot[:, :, :], tabf[:, s, :].unsqueeze(2).broadcast_to([P, TOPK, TOPK]),
                                             iota.unsqueeze(1).broadcast_to([P, TOPK, TOPK]), ALU.is_equal))
                        link(V.tensor_tensor(onehot[:, :, :], onehot[:, :, :],
                                             sidf[:, s, :].unsqueeze(1).broadcast_to([P, TOPK, TOPK]), ALU.mult))
                        link(V.tensor_reduce(tsel[:, s, :], onehot[:, :, :], AX_X, ALU.add))
                    link(V.scalar_tensor_tensor(eidf[:, :], tsel[:, 0, :], float(KEYS), tsel[:, 1, :], ALU.mult, ALU.add))
                    V.tensor_copy(eid[:, k, :], eidf[:, :]).then_inc(expert_ready, 1)
                    V.tensor_scalar(ngm[:, k:k + 1], tval[:, k, 0:1], -1.0, None, ALU.mult).then_inc(top_ready, 1)
                    assert S.n - n0 == 28, S.n - n0

                def use_row(r0, e, n_trip):
                    r = r0 + e
                    dve.wait_ge(row_full[r % ROWS], n_trip * (16 * 4 * TOPK // ROWS) + 16 * (r // ROWS + 1))
                    return rrow[:, r % ROWS, :]

                dve.wait_ge(score_a, 1)
                top(0, 1, 0)
                dve.wait_ge(ln2_in, 32)
                for b in range(BLK):
                    dve.wait_ge(h2_psum, b + 1)
                    if b == 0:
                        dve.wait_ge(score_v, 1)
                    link(V.memset(psf, 0.0))
                    base = b * PEER_HEADS * 2 * TOPK

                    def pair(i, last_one, i_sem):
                        for k in range(2):
                            r0 = base + k * 2 * TOPK
                            for e in range(TOPK):
                                row = use_row(r0, e, i_sem)
                                last = V.tensor_tensor_reduce(row, row, auxf, 1.0, 0.0, ALU.mult, ALU.add,
                                                              dots[:, k, e:e + 1])
                                last.then_inc(row_used, 1)
                            if not (last_one and k == 1):
                                top(i * 2 + (PEER_HEADS * b + k + 1), None, 1 - k)
                            dve.wait_ge(gate_exp, i_sem * 2 + (PEER_HEADS * b + k + 1))
                            link(V.reciprocal(st[:, 48 + k:49 + k], gsum[:, k:k + 1]))
                            dve.wait_ge(gelu_ready, i_sem * 2 + (PEER_HEADS * b + k + 1))
                            link(V.scalar_tensor_tensor(wgt[:, k, :], gel[:, k, :], st[:, 48 + k:49 + k],
                                                        gex[:, k, :], ALU.mult, ALU.mult))
                            for e in range(TOPK):
                                row = use_row(r0 + TOPK, e, i_sem)
                                if e:
                                    dve.wait_ge(row_used, i_sem * (4 * TOPK) + (ROWS + r0 + TOPK + e))
                                V.scalar_tensor_tensor(psf, row, wgt[:, k, e:e + 1], psf, ALU.mult, ALU.add)\
                                    .then_inc(row_used, 1)

                    with dve.Fori(0, 4 - b) as i:
                        S.enter(i, 2 * 30)
                        pair(i, False, i)
                    S.leave(4 - b)
                    if b:
                        pair(3, True, 3)
                    dve.wait_ge(row_used, ROWS + base + PEER_HEADS * 2 * TOPK)
                    if b:
                        dve.wait_ge(out_done, 16)
                    link(V.scalar_tensor_tensor(fin[:, :], gate2, 1.0, psf, ALU.add, ALU.mult))
                    link(V.scalar_tensor_tensor(fin[:, :], x1[:, b, :], ALPHA, fin[:, :], ALU.mult, ALU.add))
                    link(normalise(fin[:, :], fin[:, :], 17 + b))
                    link(V.tensor_tensor(fin[:, :], fin[:, :], ln2[:, 0, :], ALU.mult))
                    V.tensor_tensor(fin[:, :], fin[:, :], ln2[:, 1, :], ALU.add).then_inc(fin_ready, 1)

        @block.gpsimd
        def _(pool):
            G = nc.gpsimd
            S = Steps(pool, pool_step)

            def bias_rows(i, first_slab):
                for j in range(2):
                    pool.wait_ge(adarow_ready, i * 2 + (first_slab + j + 1))
                    G.dma_start(bias2[0:1, j, :], a["b_ada"][:, ds(i * 2 * W + (first_slab + j) * W, W)])\
                        .then_inc(bias_in[j], 16)


            G.memset(bias2[:, :, :], 0.0).then_inc(zeroed, 1)
            pool.wait_ge(zeroed, 1)
            bias_rows(0, 0)
            with pool.Fori(1, 4) as i:
                bias_rows(i, 0)
            if on("ssd"):
                pool.wait_ge(adt_ready, 1)
                pool.wait_ge(params_in, 16 * 17)
                pool.wait_ge(pe_used, U_SSD + 2)
                with pool.Fori(0, 4) as i:
                    S.enter(i, 4)
                    for g in range(2):
                        grp = i * 2 + g
                        hd = i * 2 * HG + g * HG
                        for k in range(4):
                            pool.wait_ge(diff_done, grp * 4 + (k + 1))
                            G.tensor_tensor(rad[:, k % 2, :, :], upper.unsqueeze(1).broadcast_to([P, 4, P]),
                                            adt[:, k // 2, ds(hd + 4 * (k % 2), 4)].unsqueeze(2).broadcast_to([P, 4, P]),
                                            ALU.mult).then_inc(rad_ready, 1)
                        pool.wait_ge(xt_ready, grp + 1)
                        v3 = lambda t: t.rearrange("p (h d) -> p h d", d=HD)
                        per_head = lambda t: t.unsqueeze(2).broadcast_to([P, HG, HD])
                        for b in range(BLK):
                            S.step(G.tensor_tensor(v3(xdt[:, b, :]), v3(x_tok[:, b, :]),
                                                   per_head(dtv[:, b, ds(hd, HG)]), ALU.mult))
                        S.wait()
                        G.tensor_tensor(v3(xend[:, :]), v3(xdt[:, 0, :]), per_head(toend[:, ds(hd, HG)]), ALU.mult)\
                            .then_inc(xdt_ready, 1)
                        for b in range(BLK):
                            last = G.tensor_tensor(v3(x_tok[:, b, :]), v3(x_tok[:, b, :]),
                                                   per_head(dskip[:, ds(hd, HG)]), ALU.mult)
                            if b:
                                last.then_inc(xskip_ready, 1)
                S.leave(4)
            if on("ada2"):
                pool.wait_ge(premix_ready, 8)
                G.memset(bias2[:, :, :], 0.0).then_inc(zeroed, 1)
                pool.wait_ge(zeroed, 2)
                bias_rows(0, 8)
                for b in range(BLK):
                    G.dma_start(x1[:, b, :], a["x"][0, b * P:(b + 1) * P, :]).then_inc(res_in, 16)
                for k, n in enumerate(("ln1_g", "ln1_b")):
                    G.dma_start(ln1[:, k, :], a[n].broadcast_to([P, D])).then_inc(res_in, 16)
                with pool.Fori(1, 8) as i:
                    bias_rows(i, 8)
            if on("all"):
                pool.wait_ge(h2_ready, BLK)
                for k, n in enumerate(("ln2_g", "ln2_b")):
                    G.dma_start(ln2[:, k, :], a[n].broadcast_to([P, D])).then_inc(ln2_in, 16)
                pool.wait_ge(pe_used, U_END + 2)
                for b in range(BLK):
                    base = b * PEER_HEADS * 2 * TOPK

                    def pair(i):
                        for k in range(2):
                            pool.wait_ge(expert_ready, i * 2 + (PEER_HEADS * b + k + 1))
                            for s, table in enumerate(("peer_u", "peer_v")):
                                for e in range(TOPK):
                                    r = base + (2 * k + s) * TOPK + e
                                    pool.wait_ge(row_used, i * (4 * TOPK) + (r + 1))
                                    pool.sem_inc(held, 1)
                                    G.indirect_dma_start(
                                        out=rrow[:, r % ROWS, :], out_offset=None, in_=a[table][0],
                                        in_offset=bass.IndirectOffsetOnAxis(ap=eid[:, k, e:e + 1], axis=0))\
                                        .then_inc(row_full[r % ROWS], 16)

                    with pool.Fori(0, 4) as i:
                        pair(i)

    return nc


INPUTS = ("x", "c", "positions", "w_ada", "b_ada", "w_in", "b_gate", "conv_w", "conv_b", "dt_bias", "A_log", "D_skip",
          "ssd_norm_w", "w_ssd_out", "q_norm_w", "w_uq", "kv_norm_w", "w_ukv", "w_mla_out", "w_mix_out",
          "ln1_g", "ln1_b", "peer_w_q", "peer_keys_1", "peer_keys_2", "peer_u", "peer_v", "ln2_g", "ln2_b")


def kernel(**inputs):
    import concourse.bacc as bacc
    from concourse.bass_utils import run_bass_kernel_spmd

    nc = bacc.Bacc("TRN2", target_bir_lowering=False, num_devices=1)
    arrays, aps = {}, {}
    for name in INPUTS + ("consts",):
        x = constants() if name == "consts" else np.ascontiguousarray(inputs[name])
        arrays[f"in_{name}"] = x
        aps[name] = nc.dram_tensor(f"in_{name}", x.shape, mybir.dt.from_np(x.dtype), kind="ExternalInput").ap()
    out = nc.dram_tensor("out", (1, SEQ, D), F32, kind="ExternalOutput").ap()
    build(nc, aps, out)
    result = run_bass_kernel_spmd(nc, [arrays], core_ids=[0])
    return result.results[0]["out"]
```

```python
import math
from contextlib import ExitStack

import numpy as np

import concourse.bass as bass
from concourse import mybir

F32 = mybir.dt.float32
F32R = mybir.dt.float32r
U32 = mybir.dt.uint32
I32 = mybir.dt.int32
ALU = mybir.AluOpType
ACT = mybir.ActivationFunctionType
AX_X = mybir.AxisListType.X
ds = bass.ds

P = 128
D = 2048
SEQ = 256
BLK = SEQ // P
DC = D // P
EPS = 1e-5
SSD_IN = 2 * D
HEADS = 64
HD = 64
GROUPS = 8
HG = HEADS // GROUPS
CONV_DIM = SSD_IN + 2 * GROUPS * P
CT = CONV_DIM // P
MLA_HEADS = 16
RANK = 512
RC = RANK // P
NOPE, ROPE, MV = 128, 64, 128
PEER_HEADS, KEYS, TOPK = 8, 128, 16
ALPHA = 2 ** 0.25
SCALE = (NOPE + ROPE) ** -0.5
W = 512
SBUF_START = 16384 - 32
QH, KVH = NOPE + ROPE, NOPE + MV
COL_Z = 0
COL_X = SSD_IN
COL_B = COL_X + SSD_IN
COL_C = COL_B + GROUPS * P
COL_DT = SSD_IN + CONV_DIM
COL_QA = COL_DT + HEADS
COL_KVA = COL_QA + RANK
COL_KR = COL_KVA + RANK
COL_G = COL_KR + ROPE

C_ID, C_UP, C_ST, C_ONE, C_MK, C_MQ, C_IOTA, C_FREQ = 0, 128, 256, 384, 512, 768, 896, 912
C_EPS = 944
C_ALL = 945

COLS_T1, COLS_T2 = 120, 248
PC_CW = (0, 48, COLS_T1, COLS_T1 + 48)
PC_C, PC_QN, PC_KVN = 96, 112, 116
PC_NW, PC_CB, PC_BG, PC_ADA = COLS_T1 + 96, COLS_T2, COLS_T2 + 48, COLS_T2 + 80
COLS_ALL = 360

U_LOW = 0
U_ATT, N_ATT = 10, 8
U_MLA, N_MLA = 42, 8
U_SSD, N_SSD = 58, 20
U_G0, N_G0 = 138, 8
U_SO, N_SO = 154, 16
U_MIX, N_MIX = 186, 8
U_WQ, N_WQ = 202, 8
U_END = 218
ADA1, ADA_MLA, ADA_SSD, ADA_ALL = 8, 4, 8, 16


def constants():
    c = np.zeros((P, C_ALL), np.float32)
    r = np.arange(P)
    c[:, C_ID:C_ID + P] = np.eye(P)
    c[:, C_UP:C_UP + P] = r[:, None] <= r[None, :]
    c[:, C_ST:C_ST + P] = r[:, None] > r[None, :]
    c[:, C_ONE:C_ONE + P] = 1.0
    c[0, C_MK + 192:C_MK + 256] = -1e30
    c[0, C_MQ:C_MQ + 64] = 1.0
    c[:, C_IOTA:C_IOTA + TOPK] = np.arange(TOPK)
    c[:, C_FREQ:C_FREQ + 32] = (10000.0 ** (-np.arange(0, ROPE, 2) / ROPE)).astype(np.float32)
    c[:, C_EPS] = EPS
    return c


class Steps:

    def __init__(self, eng, sem):
        self.eng, self.sem, self.n, self.trips = eng, sem, 0, 0

    def step(self, ins):
        self.n += 1
        ins.then_inc(self.sem, 1)

    def wait(self, but=0):
        self.eng.wait_ge(self.sem, self.trips + self.n - but)

    def link(self, ins):
        self.step(ins)
        self.wait()

    def enter(self, i, per, first=0):
        self.trips, self.per, self.at = i * per - first * per, per, self.n

    def leave(self, count):
        assert self.n - self.at == self.per, (self.n - self.at, self.per)
        self.n, self.trips = self.at + self.per * count, 0


def build(nc, a, out, stop="all"):
    ctx = ExitStack()
    with ctx:
        KB = 1024

        def at(name, offset, shape, dt=F32):
            return nc.alloc_sbuf_tensor_at(name, shape, dt, offset=SBUF_START + int(offset))

        small = [160]

        def sm(name, shape, dt=F32):
            t = at(name, small[0], shape, dt)
            small[0] += (4 * int(np.prod(shape[1:])) + 31) // 32 * 32
            assert small[0] <= 14 * KB, (name, small[0])
            return t

        def sem(name):
            return ctx.enter_context(nc.semaphore(name))

        con = sm("con", [P, C_ALL])
        cols = sm("cols", [P, COLS_ALL])
        csil = sm("csil", [P, DC])
        adacol = sm("adacol", [P, 2 * DC])
        dtb = sm("dtb", [P, HEADS])
        anegA = sm("anegA", [P, HEADS])
        dskip = sm("dskip", [P, HEADS])
        dtv = sm("dtv", [P, BLK, HEADS])
        adt = sm("adt", [P, BLK, HEADS])
        toend = sm("toend", [P, HEADS])
        fromst = sm("fromst", [P, HEADS])
        cos2 = sm("cos2", [P, BLK, ROPE])
        sin2 = sm("sin2", [P, BLK, ROPE])
        keysT = sm("keysT", [P, 2, KEYS])
        st = sm("st", [P, 64])
        acc = sm("acc", [P, 2, W])
        bn = acc[:, 1, 0:48].rearrange("p (b k n) -> p b k n", k=4, n=6)
        ident = con[:, C_ID:C_ID + P]
        upper = con[:, C_UP:C_UP + P]
        strict = con[:, C_ST:C_ST + P]

        raw = at("raw", 14 * KB, [P, 4, 4, W])
        whi = at("whi", 46 * KB, [P, 2, 4, W], F32R)
        wlo = at("wlo", 62 * KB, [P, 2, 4, W], F32R)

        h_hi = at("h_hi", 78 * KB, [P, DC, SEQ], F32R)
        h_lo = at("h_lo", 94 * KB, [P, DC, SEQ], F32R)
        adabc = at("adabc", 78 * KB, [P, 4, D])
        gate1, shift2, scale2, gate2 = (adabc[:, j, :] for j in range(4))
        premix = at("premix", 110 * KB, [P, DC, SEQ])
        h2 = at("h2", 110 * KB, [P, BLK, D])
        x_in = at("x_in", 126 * KB, [P, BLK, D])
        xnT = at("xnT", 142 * KB, [P, DC, SEQ])
        oT = at("oT", 126 * KB, [P, DC, SEQ])
        cqT_hi = at("cqT_hi", 142 * KB, [P, RC, SEQ], F32R)
        cqT_lo = at("cqT_lo", 146 * KB, [P, RC, SEQ], F32R)
        ckT_hi = at("ckT_hi", 150 * KB, [P, RC, SEQ], F32R)
        ckT_lo = at("ckT_lo", 154 * KB, [P, RC, SEQ], F32R)
        yT = at("yT", 126 * KB, [P, 2 * DC, SEQ])
        yT_lo = at("yT_lo", 126 * KB, [P, 2 * DC, SEQ], F32R)
        mx_hi = at("mx_hi", 126 * KB, [P, DC, SEQ], F32R)
        mx_lo = at("mx_lo", 142 * KB, [P, DC, SEQ], F32R)
        h2_hi = at("h2_hi", 126 * KB, [P, DC, SEQ], F32R)
        h2_lo = at("h2_lo", 142 * KB, [P, DC, SEQ], F32R)
        ada_in = at("ada_in", 174 * KB, [P, 4, 4, W])
        ada2_in = at("ada2_in", 190 * KB, [P, 4, 2, W])
        adarow = at("adarow", 206 * KB, [1, W])
        rows = at("rows", 158 * KB, [P, 3, P])
        krows = at("krows", 160 * KB, [P, 2, KEYS])
        posi = at("posi", 161 * KB, [P, BLK], I32)
        posf = at("posf", 161 * KB + 32, [P, BLK])
        ang = at("ang", 161 * KB + 64, [P, BLK, 32])
        turn = at("turn", 161 * KB + 512, [P, BLK, 32])
        angs = at("angs", 162 * KB, [P, 2, BLK, 32])
        cn = at("cn", 158 * KB, [P, BLK, RANK])
        junk = at("junk", 162 * KB, [P, RANK])
        sp = [at(f"sp{j}", 166 * KB + 512 * j, [P, BLK, HEADS]) for j in range(6)]
        krt = at("krt", 170 * KB, [P, BLK, ROPE])
        krs = at("krs", 170 * KB + 512, [P, BLK, ROPE])
        dk = at("dk", 172 * KB, [64, 2, SEQ])
        kpe2 = at("kpe2", 171 * KB, [P, BLK, 2, ROPE])
        qn = at("qn", 158 * KB, [P, 4, SEQ])
        kn = at("kn", 162 * KB, [P, 4, SEQ])
        vt = at("vt", 166 * KB, [P, BLK, 4 * MV])
        qr = at("qr", 170 * KB, [P, BLK, 4, ROPE])
        qrt = at("qrt", 172 * KB, [P, BLK, 4, ROPE])
        qrs = at("qrs", 174 * KB, [P, BLK, 4, ROPE])
        qpeT = at("qpeT", 176 * KB, [P, 2, SEQ])
        probs = at("probs", 178 * KB, [P, 4, 3 * P])
        pT = at("pT", 184 * KB, [P, 4, 3 * P])
        kpeT = at("kpeT", 125 * KB, [P, SEQ])
        oT_hi = at("oT_hi", 158 * KB, [P, DC, SEQ], F32R)
        oT_lo = at("oT_lo", 174 * KB, [P, DC, SEQ], F32R)
        xc = at("xc", 158 * KB, [P, 4, SEQ])
        bcT = at("bcT", 162 * KB, [P, 2, SEQ])
        x_tok = at("x_tok", 164 * KB, [P, BLK, W])
        xdt = at("xdt", 168 * KB, [P, BLK, W])
        xend = at("xend", 172 * KB, [P, W])
        zs = at("zs", 174 * KB, [P, BLK, W])
        yg = at("yg", 178 * KB, [P, BLK, W])
        rad = at("rad", 182 * KB, [P, 2, 4, P])
        mt = at("mt", 186 * KB, [P, BLK, HG, P])
        cbm = at("cbm", 194 * KB, [P, 3, P])
        yjunk = at("yjunk", 196 * KB, [P, W])
        g0 = at("g0", 192 * KB, [P, DC, SEQ])
        yT_hi = at("yT_hi", 158 * KB, [P, 2 * DC, SEQ], F32R)
        gtmp = at("gtmp", 190 * KB, [P, W])
        x1 = at("x1", 158 * KB, [P, BLK, D])
        ln1 = at("ln1", 174 * KB, [P, 2, D])
        mtmp = at("mtmp", 190 * KB, [P, W])
        qT = at("qT", 192 * KB, [P, DC, SEQ])
        ln2 = at("ln2", 174 * KB, [P, 2, D])
        ROWS = 8
        rrow = at("rrow", 14 * KB, [P, ROWS, D])
        score = at("score", 78 * KB, [P, BLK * PEER_HEADS, 2 * KEYS])
        scur = at("scur", 94 * KB, [P, 2, KEYS])
        swork = at("swork", 95 * KB, [P, 2, KEYS])
        cand = at("cand", 96 * KB, [P, TOPK, TOPK])
        cwork = at("cwork", 97 * KB, [P, TOPK * TOPK])
        onehot = at("onehot", 98 * KB, [P, TOPK, TOPK])
        pk = lambda name, k, shape, dt=F32: at(name, 99 * KB + 128 * k, shape, dt)
        sval = pk("sval", 0, [P, 2, TOPK])
        sidx = pk("sidx", 1, [P, 2, TOPK], U32)
        sidf = pk("sidf", 2, [P, 2, TOPK])
        tpos = pk("tpos", 3, [P, TOPK], U32)
        tab = pk("tab", 4, [P, 2, TOPK], U32)
        tabf = pk("tabf", 5, [P, 2, TOPK])
        tsel = pk("tsel", 6, [P, 2, TOPK])
        tval = pk("tval", 7, [P, 2, TOPK])
        eidf = pk("eidf", 8, [P, TOPK])
        eid = pk("eid", 9, [P, 2, TOPK], U32)
        ngm = pk("ngm", 10, [P, 2])
        gex = pk("gex", 11, [P, 2, TOPK])
        gsum = pk("gsum", 12, [P, 2])
        dots = pk("dots", 13, [P, 2, TOPK])
        gel = pk("gel", 14, [P, 2, TOPK])
        wgt = pk("wgt", 15, [P, 2, TOPK])
        fin = at("fin", 192 * KB, [P, D])

        ps = ctx.enter_context(nc.psum_tensor("ps", [P, 2, 2, W], F32))
        aux = ctx.enter_context(nc.psum_tensor("aux", [P, 4, W], F32))
        auxf = aux[:, :, :].rearrange("p b n -> p (b n)")
        psf = ps[:, :, :, :].rearrange("p a b n -> p (a b n)")

        raw_full = [sem(f"raw_full{j}") for j in range(4)]
        hi_ready = sem("hi_ready")
        lo_ready = sem("lo_ready")
        pe_used = sem("pe_used")
        params_in = sem("params_in")
        x_loaded = sem("x_loaded")
        ada_full = [sem(f"ada_full{j}") for j in range(4)]
        ada_used = sem("ada_used")
        acc_ready = sem("acc_ready")
        acc_summed = sem("acc_summed")
        ada2_full = [sem(f"ada2_full{j}") for j in range(4)]
        ada2_used = sem("ada2_used")
        ada3_full = [sem(f"ada3_full{j}") for j in range(2)]
        ada3_used = sem("ada3_used")
        bias_in = sem("bias_in")
        row_ready = sem("row_ready")
        row_stored = sem("row_stored")
        ada_in_ready = sem("ada_in_ready")
        rows_turned = sem("rows_turned")
        cols_ready = sem("cols_ready")
        c_hi_ready = sem("c_hi_ready")
        c_ready = sem("c_ready")
        x_normed = sem("x_normed")
        x_turned = sem("x_turned")
        xT_ready = sem("xT_ready")
        angles_ready = sem("angles_ready")
        sines_ready = sem("sines_ready")
        h_full = sem("h_full")
        h_hi_ready = sem("h_hi_ready")
        h_ready = sem("h_ready")
        sumsq_ready = sem("sumsq_ready")
        cn_ready = sem("cn_ready")
        cn_turned = sem("cn_turned")
        cn_hi_ready = sem("cn_hi_ready")
        cn_split = sem("cn_split")
        sp_x = sem("sp_x")
        sp_e = sem("sp_e")
        neg_a = sem("neg_a")
        adt_ready = sem("adt_ready")
        cum_ready = sem("cum_ready")
        decay_ready = sem("decay_ready")
        dk_copied = sem("dk_copied")
        dk_turned = sem("dk_turned")
        kpe_ready = sem("kpe_ready")
        kpe_turned = sem("kpe_turned")
        kpe_read = sem("kpe_read")
        att_evac_a = sem("att_evac_a")
        att_evac_v = sem("att_evac_v")
        qr_copied = sem("qr_copied")
        qr_ready = sem("qr_ready")
        qpe_turned = sem("qpe_turned")
        qpe_read = sem("qpe_read")
        scores_done = sem("scores_done")
        negmax_ready = sem("negmax_ready")
        exp_done = sem("exp_done")
        probs_ready = sem("probs_ready")
        probs_turned = sem("probs_turned")
        pT_a = sem("pT_a")
        pT_v = sem("pT_v")
        pv_done = sem("pv_done")
        o_read = sem("o_read")
        o_hi_ready = sem("o_hi_ready")
        o_split = sem("o_split")
        b_free = sem("b_free")
        conv_done = sem("conv_done")
        silu_done = sem("silu_done")
        xt_turned = sem("xt_turned")
        xt_ready = sem("xt_ready")
        xdt_ready = sem("xdt_ready")
        xskip_ready = sem("xskip_ready")
        rad_ready = sem("rad_ready")
        cb_done = sem("cb_done")
        cb_read = sem("cb_read")
        diff_done = sem("diff_done")
        decay_exp = sem("decay_exp")
        mt_ready = sem("mt_ready")
        y_done = sem("y_done")
        z_silu = sem("z_silu")
        yg_ready = sem("yg_ready")
        ysq_ready = sem("ysq_ready")
        ytok_ready = sem("ytok_ready")
        g0_ready = sem("g0_ready")
        yt_turned = sem("yt_turned")
        yt_stored = sem("yt_stored")
        yt_hi = sem("yt_hi")
        yt_split = sem("yt_split")
        premix_ready = sem("premix_ready")
        mx_hi_ready = sem("mx_hi_ready")
        mx_split = sem("mx_split")
        res_in = sem("res_in")
        h2_ready = sem("h2_ready")
        h2_turned = sem("h2_turned")
        h2_hi_ready = sem("h2_hi_ready")
        h2_split = sem("h2_split")
        qT_a = sem("qT_a")
        qT_v = sem("qT_v")
        score_done = sem("score_done")
        score_a = sem("score_a")
        score_v = sem("score_v")
        h2_psum = sem("h2_psum")
        ln2_in = sem("ln2_in")
        expert_ready = sem("expert_ready")
        top_ready = sem("top_ready")
        gate_exp = sem("gate_exp")
        gelu_ready = sem("gelu_ready")
        row_full = [sem(f"row_full{j}") for j in range(ROWS)]
        row_used = sem("row_used")
        offset_ready = sem("offset_ready")
        normed = sem("normed")
        x1_ready = sem("x1_ready")
        var_ready = sem("var_ready")
        std_ready = sem("std_ready")
        fin_ready = sem("fin_ready")
        out_done = sem("out_done")
        held = sem("held")
        dve_step = sem("dve_step")
        act_step = sem("act_step")
        pool_step = sem("pool_step")
        probe_done = sem("probe_done")

        def kview(w):
            return w[0].rearrange("(kc p) n -> p kc n", p=P)

        w_ada, w_in = kview(a["w_ada"]), kview(a["w_in"])
        w_uq, w_ukv = kview(a["w_uq"]), kview(a["w_ukv"])
        w_so, w_mo = kview(a["w_ssd_out"]), kview(a["w_mla_out"])
        w_mix, w_pq = kview(a["w_mix_out"]), kview(a["peer_w_q"])

        ada_rows = nc.dram_tensor("ada_rows", (1, ADA_ALL * W), F32, kind="Internal").ap()

        order = ["setup", "low", "att", "mla", "ssd", "g0", "so", "mix", "h2", "wq", "all"]
        upto = order.index(stop)

        def on(phase):
            return order.index(phase) <= upto

        last_unit = {"setup": U_LOW, "low": U_ATT, "att": U_MLA, "mla": U_SSD, "ssd": U_G0, "g0": U_SO,
                     "so": U_MIX, "mix": U_WQ, "h2": U_WQ, "wq": U_END, "all": U_END}[stop]

        def full_count(base, j, i, per):
            return 16 * ((base + j) // 4 + 1) + i * (16 * (per // 4))

        block = ctx.enter_context(nc.Block())

        @block.sync
        def _(sp_):
            def load(base, j, i, per, src):
                n = base + j
                sp_.wait_ge(lo_ready, i * per + (n + 1))
                sp_.sem_inc(held, 1)
                kcs, width = src.shape[1:]
                dst = raw[:, n % 4, :, 0:width] if kcs == 4 else \
                    raw[:, n % 4].rearrange("p a b -> p (a b)")[:, 0:kcs * width].rearrange(
                        "p (kc n) -> p kc n", kc=kcs)
                sp_.dma_start(dst, src).then_inc(raw_full[n % 4], 16)

            def small_in(dst, src):
                sp_.dma_start(dst, src).then_inc(params_in, 16)

            def rowsof(ap, first, n):
                return ap.rearrange("a (r p) -> (a r) p", p=P)[first:first + n, :]

            small_in(rows[PC_C:PC_C + DC, 0, :], rowsof(a["c"], 0, DC))
            for j in range(4):
                small_in(rows[48 * (j % 2):48 * (j % 2) + 48, j // 2, :], rowsof(a["conv_w"][0], j * CT, CT))
            small_in(rows[PC_QN:PC_QN + RC, 0, :], rowsof(a["q_norm_w"], 0, RC))
            small_in(rows[PC_KVN:PC_KVN + RC, 0, :], rowsof(a["kv_norm_w"], 0, RC))
            small_in(rows[96:96 + 2 * DC, 1, :], rowsof(a["ssd_norm_w"], 0, 2 * DC))
            small_in(rows[0:CT, 2, :], rowsof(a["conv_b"], 0, CT))
            small_in(rows[CT:CT + 2 * DC, 2, :], rowsof(a["b_gate"], 0, 2 * DC))
            small_in(rows[CT + 2 * DC:CT + 4 * DC, 2, :], rowsof(a["b_ada"], 0, 2 * DC))
            small_in(con[:, :], a["consts"])
            small_in(krows[:, 0, :], a["peer_keys_1"][0])
            small_in(krows[:, 1, :], a["peer_keys_2"][0])
            with nc.allow_non_contiguous_dma(reason="256 positions, one for each token"):
                small_in(posi[:, :], a["positions"].rearrange("b (t p) -> p (b t)", p=P))
            small_in(dtb[:, :], a["dt_bias"].broadcast_to([P, HEADS]))
            small_in(anegA[:, :], a["A_log"].broadcast_to([P, HEADS]))
            small_in(dskip[:, :], a["D_skip"].broadcast_to([P, HEADS]))

            def ada1_unit(i, u):
                sp_.wait_ge(ada_used, i * 8 + (u + 1))
                sp_.sem_inc(held, 1)
                sp_.dma_start(ada_in[:, u % 4], w_ada[:, 4 * (u % 4):4 * (u % 4) + 4, ds(i * 2 * W + (u // 4) * W, W)])\
                    .then_inc(ada_full[u % 4], 16)

            for u in range(4):
                ada1_unit(0, u)
            for b in range(BLK):
                sp_.dma_start(x_in[:, b, :], a["x"][0, b * P:(b + 1) * P, :]).then_inc(x_loaded, 16)
            for u in range(4, 8):
                ada1_unit(0, u)
            with sp_.Fori(1, 4) as i:
                for u in range(8):
                    ada1_unit(i, u)


            if on("low"):
                for s, col in enumerate((COL_QA, COL_KVA)):
                    for q in range(4):
                        load(U_LOW, 4 * s + q, 0, 0, w_in[:, 4 * q:4 * q + 4, col:col + W])
                for k, col in enumerate((COL_DT, COL_KR)):
                    load(U_LOW, 8 + k, 0, 0, w_in[:, :, col:col + 64])
            if on("att"):
                with sp_.Fori(0, 4) as i:
                    for k in range(2):
                        load(U_ATT, k, i, N_ATT, w_uq[:, :, ds(i * 4 * QH + k * 2 * QH, 2 * QH)])
                    for k in range(2):
                        load(U_ATT, 2 + k, i, N_ATT, w_ukv[:, :, ds(i * 4 * KVH + k * 2 * KVH, 2 * KVH)])
                    for q in range(4):
                        load(U_ATT, 4 + q, i, N_ATT, w_in[:, 4 * q:4 * q + 4, ds(i * W + (COL_G + D), W)])
            if on("mla"):
                with sp_.Fori(0, 2) as i:
                    for u in range(8):
                        load(U_MLA, u, i, N_MLA, w_mo[:, 4 * (u % 4):4 * (u % 4) + 4, ds(i * 2 * W + (u // 4) * W, W)])
            if on("ssd"):
                with sp_.Fori(0, 4) as i:
                    for g in range(2):
                        for q in range(4):
                            load(U_SSD, 10 * g + q, i, N_SSD,
                                 w_in[:, 4 * q:4 * q + 4, ds(i * 2 * W + (COL_X + g * W), W)])
                        for k, col in enumerate((COL_B, COL_C)):
                            load(U_SSD, 10 * g + 4 + k, i, N_SSD, w_in[:, :, ds(i * 2 * P + (col + g * P), P)])
                        for q in range(4):
                            load(U_SSD, 10 * g + 6 + q, i, N_SSD,
                                 w_in[:, 4 * q:4 * q + 4, ds(i * 2 * W + (COL_Z + g * W), W)])
            if on("g0"):
                with sp_.Fori(0, 2) as i:
                    for u in range(8):
                        load(U_G0, u, i, N_G0,
                             w_in[:, 4 * (u % 4):4 * (u % 4) + 4, ds(i * 2 * W + COL_G + (u // 4) * W, W)])
            if on("so"):
                with sp_.Fori(0, 2) as i:
                    for u in range(16):
                        load(U_SO, u, i, N_SO,
                             w_so[:, 4 * (u % 8):4 * (u % 8) + 4, ds(i * 2 * W + (u // 8) * W, W)])
            if on("mix"):
                with sp_.Fori(0, 2) as i:
                    for u in range(8):
                        load(U_MIX, u, i, N_MIX, w_mix[:, 4 * (u % 4):4 * (u % 4) + 4, ds(i * 2 * W + (u // 4) * W, W)])
            if on("wq"):
                with sp_.Fori(0, 2) as i:
                    for u in range(8):
                        load(U_WQ, u, i, N_WQ, w_pq[:, 4 * (u % 4):4 * (u % 4) + 4, ds(i * 2 * W + (u // 4) * W, W)])
            if not on("wq"):
                for k in range(2):
                    load(last_unit, k, 0, 0, w_in[:, 0:4, 0:W])
            if on("all"):
                for b in range(BLK):
                    sp_.wait_ge(fin_ready, b + 1)
                    sp_.dma_start(out[0, b * P:(b + 1) * P, :], fin[:, :]).then_inc(out_done, 16)
                sp_.wait_ge(out_done, 16 * BLK)

        @block.tensor
        def _(pe):
            mm = nc.tensor.matmul

            def wait_unit(base, j, i, per):
                pe.wait_ge(lo_ready, i * per + (base + j + 5))

            def token_unit(base, j, i, per, x_hi, x_lo, k0, klast, outs, width=W, kcs=4, used=True):
                wait_unit(base, j, i, per)
                n = (base + j) % 2
                hi, lo = whi[:, n], wlo[:, n]
                if kcs != 4:
                    hi, lo = (w.rearrange("p a b -> p (a b)")[:, 0:kcs * width].rearrange(
                        "p (kc n) -> p kc n", kc=kcs) for w in (hi, lo))
                for kc in range(kcs):
                    k = k0 + kc
                    for b in range(BLK):
                        t = slice(b * P, b * P + P)
                        mm(outs[b], x_hi[:, k, t], hi[:, kc, 0:width], start=(k == 0), stop=False)
                        mm(outs[b], x_lo[:, k, t], hi[:, kc, 0:width], start=False, stop=False)
                        last = mm(outs[b], x_hi[:, k, t], lo[:, kc, 0:width], start=False, stop=(k == klast))
                if used:
                    last.then_inc(pe_used, 1)

            def channel_unit(base, j, i, per, x_hi, x_lo, k0, klast, tiles, kcs=4, used=True, width=P):
                wait_unit(base, j, i, per)
                n = (base + j) % 2
                hi, lo = whi[:, n], wlo[:, n]
                if kcs != 4:
                    hi, lo = (w.rearrange("p a b -> p (a b)")[:, 0:kcs * width].rearrange(
                        "p (kc n) -> p kc n", kc=kcs) for w in (hi, lo))
                for kc in range(kcs):
                    k = k0 + kc
                    for o, c, first in tiles:
                        wh, wl = hi[:, kc, c:c + width], lo[:, kc, c:c + width]
                        mm(o, wh, x_hi[:, k, :], start=(k == 0 and first), stop=False, skip_group_check=True)
                        mm(o, wh, x_lo[:, k, :], start=False, stop=False, skip_group_check=True)
                        last = mm(o, wl, x_hi[:, k, :], start=False, stop=(k == klast), skip_group_check=True)
                if used:
                    last.then_inc(pe_used, 1)

            def slab_tiles(buf):
                return [(ps[:, buf, t // 2, (t % 2) * SEQ:(t % 2) * SEQ + SEQ], t * P, t % 2 == 0) for t in range(4)]

            pe.sem_inc(pe_used, 2)
            pe.sem_inc(diff_done, 2)
            pe.sem_inc(acc_summed, 2)

            pe.wait_ge(params_in, 16 * 18)
            for j, (first, n) in enumerate(((0, COLS_T1), (COLS_T1, P), (COLS_T2, COLS_ALL - COLS_T2))):
                last = nc.tensor.transpose(aux[:, 0, first:first + n], rows[0:n, j, :], ident[0:n, 0:n])
            last.then_inc(rows_turned, 1)
            for j in range(2):
                last = nc.tensor.transpose(aux[:, 1, j * P:j * P + P], krows[:, j, :], ident)
            last.then_inc(rows_turned, 1)
            pe.wait_ge(x_normed, BLK)
            pe.wait_ge(cols_ready, 2)
            for r in range(4):
                if r >= 2:
                    pe.wait_ge(xT_ready, r - 1)
                for k in range(4):
                    for b in range(BLK):
                        last = nc.tensor.transpose(
                            aux[:, 2 * (r % 2) + k // 2, (k % 2) * SEQ + b * P:(k % 2) * SEQ + b * P + P],
                            x_in[:, b, (4 * r + k) * P:(4 * r + k) * P + P], ident)
                last.then_inc(x_turned, 1)
            for k in range(ADA1):
                pe.wait_ge(acc_ready, k + 1)
                for t in range(4):
                    last = mm(ps[:, 1, 1, 4 * k + t:4 * k + t + 1], acc[:, k % 2, t * P:t * P + P],
                              con[:, C_ONE:C_ONE + 1], start=True, stop=True)
                last.then_inc(acc_summed, 1)

            def sum_slab(bank, k, slab):
                pe.wait_ge(acc_ready, ADA1 + 1 + slab)
                mm(bank[0:1, :], con[:, C_ONE:C_ONE + 1], acc[:, k, :], start=True, stop=True).then_inc(acc_summed, 1)

            if on("low"):
                def turn_cn(s):
                    pe.wait_ge(cn_ready, s + 1)
                    for t in range(RC):
                        for b in range(BLK):
                            last = nc.tensor.transpose(
                                aux[:, 2 * s + t // 2, (t % 2) * SEQ + b * P:(t % 2) * SEQ + b * P + P],
                                cn[:, b, t * P:t * P + P], ident)
                    last.then_inc(cn_turned, 1)

                for s in range(2):
                    for q in range(4):
                        if s == 0:
                            pe.wait_ge(h_ready, q + 1)
                        token_unit(U_LOW, 4 * s + q, 0, 0, h_hi, h_lo, 4 * q, DC - 1,
                                   [ps[:, s, b, :] for b in range(BLK)])
                        if (s, q) == (1, 2):
                            turn_cn(0)
                for k in range(2):
                    channel_unit(U_LOW, 8 + k, 0, 0, h_hi, h_lo, 0, DC - 1,
                                 [(ps[0:64, 0, k, 0:SEQ], 0, True)], kcs=DC, width=64)
                    if k == 0:
                        turn_cn(1)
                for k in range(2):
                    pe.wait_ge(dk_copied, k + 1)
                    for b in range(BLK):
                        last = nc.tensor.transpose(aux[:, b, 64 * k:64 * k + 64], dk[:, k, b * P:b * P + P],
                                                   ident[0:64, 0:64])
                    last.then_inc(dk_turned, 1)
                pe.wait_ge(kpe_ready, 1)
                for b in range(BLK):
                    last = nc.tensor.transpose(aux[:, 3, b * P:b * P + P],
                                               kpe2[:, b, :, :].rearrange("p a b -> p (a b)"), ident)
                last.then_inc(kpe_turned, 1)
            if on("att"):
                pe.wait_ge(cn_split, 2)
                pe.wait_ge(kpe_read, 1)
                with pe.Fori(0, 4) as i:
                    for k in range(2):
                        if k == 1:
                            pe.wait_ge(row_ready, i + 1)
                        channel_unit(U_ATT, k, i, N_ATT, cqT_hi, cqT_lo, 0, RC - 1,
                                     [(ps[:, 1, k, e * SEQ:e * SEQ + SEQ], e * QH, e == 0) for e in range(2)], used=False)
                        if k == 0:
                            pe.wait_ge(b_free, i + 1)
                        n = (U_ATT + k) % 2
                        rope = [w[:, n, :, 0:2 * QH].rearrange("p kc (e m) -> p kc e m", e=2)[:, :, :, NOPE:QH]
                                for w in (whi, wlo)]
                        for b in range(BLK):
                            o = ps[:, 0, 0, b * 256 + k * P:b * 256 + k * P + P]
                            t = slice(b * P, b * P + P)
                            for kc in range(RC):
                                mm(o, cqT_hi[:, kc, t], rope[0][:, kc], start=(kc == 0), stop=False)
                                mm(o, cqT_lo[:, kc, t], rope[0][:, kc], start=False, stop=False)
                                last = mm(o, cqT_hi[:, kc, t], rope[1][:, kc], start=False, stop=(kc == RC - 1))
                        last.then_inc(pe_used, 1)
                    for k in range(2):
                        channel_unit(U_ATT, 2 + k, i, N_ATT, ckT_hi, ckT_lo, 0, RC - 1,
                                     [(aux[:, 2 + k, e * SEQ:e * SEQ + SEQ], e * KVH, e == 0) for e in range(2)],
                                     used=False)
                        n = (U_ATT + 2 + k) % 2
                        val = [w[:, n, :, :].rearrange("p kc (e m) -> p kc e m", e=2)[:, :, :, NOPE:KVH]
                               for w in (whi, wlo)]
                        for b in range(BLK):
                            o = aux[:, b, k * 256:k * 256 + 256]
                            t = slice(b * P, b * P + P)
                            for kc in range(RC):
                                mm(o, ckT_hi[:, kc, t], val[0][:, kc], start=(kc == 0), stop=False)
                                mm(o, ckT_lo[:, kc, t], val[0][:, kc], start=False, stop=False)
                                last = mm(o, ckT_hi[:, kc, t], val[1][:, kc], start=False, stop=(kc == RC - 1))
                        last.then_inc(pe_used, 1)
                    pe.wait_ge(qr_ready, i + 1)
                    for pair in range(2):
                        for b in range(BLK):
                            last = nc.tensor.transpose(
                                ps[:, 1, 0, pair * SEQ + b * P:pair * SEQ + b * P + P],
                                qr[:, b, 2 * pair:2 * pair + 2, :].rearrange("p a b -> p (a b)"), ident)
                    last.then_inc(qpe_turned, 1)
                    channel_unit(U_ATT, 4, i, N_ATT, h_hi, h_lo, 0, DC - 1, slab_tiles(0))
                    pe.wait_ge(att_evac_a, i + 1)
                    pe.wait_ge(att_evac_v, i + 1)
                    pe.wait_ge(qpe_read, i + 1)
                    for h in range(4):
                        r = slice(64 * (h % 2), 64 * (h % 2) + 64)
                        for b in range(BLK):
                            nk = P * (b + 1)
                            o = aux[:, h, b * P:b * P + nk]
                            t = slice(b * P, b * P + P)
                            mm(o, qn[:, h, t], kn[:, h, 0:nk], start=True, stop=False)
                            mm(o, qpeT[r, h // 2, t], kpeT[r, 0:nk], start=False, stop=False)
                            last = mm(o, con[0:1, C_MQ:C_MQ + P], con[0:1, C_MK + 256 - nk:C_MK + 256],
                                      start=False, stop=True)
                    last.then_inc(scores_done, 1)
                    channel_unit(U_ATT, 5, i, N_ATT, h_hi, h_lo, 4, DC - 1, slab_tiles(0))
                    channel_unit(U_ATT, 6, i, N_ATT, h_hi, h_lo, 8, DC - 1, slab_tiles(0))
                    pe.wait_ge(probs_ready, i + 1)
                    for h in range(4):
                        for k in range(3):
                            last = nc.tensor.transpose(aux[:, h, k * P:k * P + P], probs[:, h, k * P:k * P + P], ident)
                        last.then_inc(probs_turned, 1)
                    channel_unit(U_ATT, 7, i, N_ATT, h_hi, h_lo, 12, DC - 1, slab_tiles(0))
                    for h in range(4):
                        pe.wait_ge(pT_v if h % 2 else pT_a, i * 2 + (h // 2 + 1))
                        v0, v1 = (vt[:, b, h * MV:h * MV + MV] for b in range(BLK))
                        mm(aux[:, h, 0:P], v0, pT[:, h, 0:P], start=True, stop=True)
                        mm(aux[:, h, P:2 * P], v0, pT[:, h, P:2 * P], start=True, stop=False)
                        last = mm(aux[:, h, P:2 * P], v1, pT[:, h, 2 * P:3 * P], start=False, stop=True)
                    last.then_inc(pv_done, 1)
                    sum_slab(ps[:, 1, 1, :], 0, i)
            if on("mla"):
                pe.wait_ge(adt_ready, 1)
                pe.wait_ge(o_read, 4)
                mm(aux[:, 2, 0:HEADS], strict, adt[:, 0, :], start=True, stop=True)
                mm(aux[:, 2, HEADS:2 * HEADS], upper, adt[:, 1, :], start=True, stop=True).then_inc(cum_ready, 1)
                with pe.Fori(0, 2) as i:
                    pe.wait_ge(row_ready, i * 2 + (ADA_MLA + 1))
                    for s in range(2):
                        for q in range(4):
                            pe.wait_ge(o_split, q + 1)
                            channel_unit(U_MLA, 4 * s + q, i, N_MLA, oT_hi, oT_lo, 4 * q, DC - 1, slab_tiles(1 - s))
                        if s:
                            pe.wait_ge(row_ready, i * 2 + (ADA_MLA + 2))
                        sum_slab(aux[:, 0, :], 0, i * 2 + (ADA_MLA + s))
            if on("ssd"):
                def ssd_pair(i, first):
                    for g in range(2):
                        u, bx, bb = 10 * g, 1 - g, g
                        grp = i * 2 + g

                        def log_decays(ks):
                            for k in ks:
                                pe.wait_ge(rad_ready, grp * 4 + (k + 1))
                                if k >= 2:
                                    pe.wait_ge(decay_exp, grp * 4 + (k - 1))
                                mm(aux[:, 3 - k % 2, :], strict, rad[:, k % 2, :, :].rearrange("p h l -> p (h l)"),
                                   start=True, stop=True).then_inc(diff_done, 1)

                        for q in range(4):
                            channel_unit(U_SSD, u + q, i, N_SSD, h_hi, h_lo, 4 * q, DC - 1, slab_tiles(bx))
                            if q == 2:
                                pe.wait_ge(row_ready, grp + (ADA_SSD + 1))
                                if not (first and g == 0):
                                    turn_y(grp)
                                log_decays((0, 1))
                            if q == 3:
                                log_decays((2, 3))
                        for k in range(2):
                            channel_unit(U_SSD, u + 4 + k, i, N_SSD, h_hi, h_lo, 0, DC - 1,
                                         [(ps[:, bb, k, 0:SEQ], 0, True)], kcs=DC)
                        zout = [ps[:, bx, b, :] for b in range(BLK)]
                        token_unit(U_SSD, u + 6, i, N_SSD, h_hi, h_lo, 0, DC - 1, zout)
                        pe.wait_ge(silu_done, grp * 5 + 4)
                        if not (first and g == 0):
                            pe.wait_ge(yt_stored, grp)
                        for t in range(4):
                            for b in range(BLK):
                                last = nc.tensor.transpose(aux[:, b, t * P:t * P + P], xc[:, t, b * P:b * P + P], ident)
                        last.then_inc(xt_turned, 1)
                        token_unit(U_SSD, u + 7, i, N_SSD, h_hi, h_lo, 4, DC - 1, zout)
                        pe.wait_ge(silu_done, grp * 5 + 5)
                        pe.wait_ge(decay_exp, grp * 4 + 4)
                        for k, (s, l) in enumerate(((0, 0), (1, 1), (0, 1))):
                            last = mm(aux[:, 2, k * P:k * P + P], bcT[:, 0, s * P:s * P + P],
                                      bcT[:, 1, l * P:l * P + P], start=True, stop=True)
                        last.then_inc(cb_done, 1)
                        token_unit(U_SSD, u + 8, i, N_SSD, h_hi, h_lo, 8, DC - 1, zout)
                        token_unit(U_SSD, u + 9, i, N_SSD, h_hi, h_lo, 12, DC - 1, zout)
                        pe.wait_ge(xdt_ready, grp + 1)
                        pe.wait_ge(mt_ready, grp * 4 + 4)
                        for b in range(BLK):
                            for h in range(HG):
                                mm(aux[:, b, h * HD:h * HD + HD], mt[:, b, h, :], xdt[:, b, h * HD:h * HD + HD],
                                   start=True, stop=True)
                        mm(aux[:, 3, :], cbm[:, 2, :], xend[:, :], start=True, stop=True).then_inc(y_done, 1)
                        sum_slab(aux[:, 2, :], 0, grp + ADA_SSD)

                def turn_y(number):
                    pe.wait_ge(ytok_ready, number)
                    for t in range(4):
                        for b in range(BLK):
                            last = nc.tensor.transpose(
                                aux[:, t // 2, (t % 2) * SEQ + b * P:(t % 2) * SEQ + b * P + P],
                                yg[:, b, t * P:t * P + P], ident)
                    last.then_inc(yt_turned, 1)

                ssd_pair(0, True)
                with pe.Fori(1, 4) as i:
                    ssd_pair(i, False)
            if on("g0"):
                for s in range(4):
                    for q in range(4):
                        channel_unit(U_G0, 4 * s + q, 0, 0, h_hi, h_lo, 4 * q, DC - 1, slab_tiles(1 - s % 2))
                        if (s, q) == (0, 2):
                            turn_y(GROUPS)
            if on("so"):
                with pe.Fori(0, 2) as i:
                    for s in range(2):
                        for q in range(8):
                            pe.wait_ge(yt_split, q // 2 + 1)
                            channel_unit(U_SO, 8 * s + q, i, N_SO, yT_hi, yT_lo, 4 * q, 2 * DC - 1, slab_tiles(1 - s))
            if on("mix"):
                with pe.Fori(0, 2) as i:
                    for s in range(2):
                        for q in range(4):
                            pe.wait_ge(mx_split, q + 1)
                            token_unit(U_MIX, 4 * s + q, i, N_MIX, mx_hi, mx_lo, 4 * q, DC - 1,
                                       [ps[:, 1 - s, b, :] for b in range(BLK)])
            if on("h2"):
                for b in range(BLK):
                    pe.wait_ge(h2_ready, b + 1)
                    for t in range(DC):
                        last = nc.tensor.transpose((auxf, psf)[b][:, t * P:t * P + P], h2[:, b, t * P:t * P + P], ident)
                    last.then_inc(h2_turned, 1)
            if on("wq"):
                pe.wait_ge(h2_split, BLK)
                def scores(s):
                    pe.wait_ge(qT_a, s + 1)
                    pe.wait_ge(qT_v, s + 1)
                    if s >= 2:
                        pe.wait_ge(score_a, s - 1)
                        pe.wait_ge(score_v, s - 1)
                    for b in range(BLK):
                        for t in range(4):
                            last = mm(aux[:, 2 * (s % 2) + b, t * KEYS:t * KEYS + KEYS],
                                      qT[:, 4 * s + t, b * P:b * P + P], keysT[:, t % 2, :], start=True, stop=True)
                    last.then_inc(score_done, 1)

                for s in range(4):
                    for q in range(4):
                        channel_unit(U_WQ, 4 * s + q, 0, 0, h2_hi, h2_lo, 4 * q, DC - 1, slab_tiles(1 - s % 2))
                        if s and q == 1:
                            scores(s - 1)
                scores(3)

        @block.scalar
        def _(act):
            F = nc.scalar.activation
            S = Steps(act, act_step)

            def hi(base, j, i, per, cols_=W):
                n = base + j
                act.wait_ge(raw_full[n % 4], full_count(base, j, i, per))
                act.wait_ge(pe_used, i * per + (n + 1))
                F(whi[:, n % 2, :, 0:cols_], raw[:, n % 4, :, 0:cols_], ACT.Copy).then_inc(hi_ready, 1)

            def hi_flat(base, j, i, per, count):
                n = base + j
                act.wait_ge(raw_full[n % 4], full_count(base, j, i, per))
                act.wait_ge(pe_used, i * per + (n + 1))
                F(whi[:, n % 2].rearrange("p a b -> p (a b)")[:, 0:count],
                  raw[:, n % 4].rearrange("p a b -> p (a b)")[:, 0:count], ACT.Copy).then_inc(hi_ready, 1)

            def slab_done(base, j, i, per):
                act.wait_ge(pe_used, i * per + (base + j + 3))

            def root(dst, src, scale):
                F(dst, src, ACT.Sqrt, bias=con[:, C_EPS:C_EPS + 1], scale=scale).then_inc(std_ready, 1)

            def norm_root(number, b=0):
                act.wait_ge(var_ready, number)
                root(st[:, 46 + 4 * b:47 + 4 * b], st[:, 45 + 4 * b:46 + 4 * b], 1.0)

            def apply_norm(dst, src, b, number):
                act.wait_ge(offset_ready, number)
                F(dst, src, ACT.Identity, bias=st[:, 47 + 4 * b:48 + 4 * b], scale=st[:, 46 + 4 * b:47 + 4 * b])\
                    .then_inc(normed, 1)

            act.wait_ge(cols_ready, 1)
            F(csil[:, :], cols[:, PC_C:PC_C + DC], ACT.Silu).then_inc(c_ready, 1)
            act.wait_ge(params_in, 16 * 18)
            F(anegA[:, :], anegA[:, :], ACT.Exp).then_inc(neg_a, 1)
            for b in range(BLK):
                norm_root(b + 1)
            for r in range(4):
                act.wait_ge(x_turned, r + 1)
                F(xnT[:, 4 * r:4 * r + 4, :].rearrange("p k t -> p (k t)"),
                  auxf[:, 1024 * (r % 2):1024 * (r % 2) + 1024], ACT.Copy).then_inc(xT_ready, 1)
            act.wait_ge(angles_ready, 1)
            for k, tab_ in enumerate((sin2, cos2)):
                for e in range(2):
                    last = F(tab_[:, :, 32 * e:32 * e + 32], angs[:, k], ACT.Sin)
                    last.then_inc(sines_ready, 1)
            for u in range(2):
                hi(U_LOW, u, 0, 0)
            for q in range(4):
                act.wait_ge(h_full, q + 1)
                F(h_hi[:, 4 * q:4 * q + 4, :], xnT[:, 4 * q:4 * q + 4, :], ACT.Copy).then_inc(h_hi_ready, 1)
            if on("low"):
                def sumsq(s):
                    for b in range(BLK):
                        if s or b:
                            act.wait_ge(sumsq_ready, 2 * s + b)
                        F(junk[:, :], ps[:, s, b, :], ACT.Square, accum_out=st[:, 32 + 2 * s + b:33 + 2 * s + b])\
                            .then_inc(sumsq_ready, 1)
                    act.wait_ge(sumsq_ready, 2 * s + 2)
                    root(st[:, 36 + 2 * s:38 + 2 * s], st[:, 32 + 2 * s:34 + 2 * s], 1.0 / RANK)

                def split_cn(s, norm_col, dst):
                    act.wait_ge(cn_turned, s + 1)
                    for t in range(RC):
                        F(dst[:, t, :], auxf[:, 1024 * s + t * SEQ:1024 * s + (t + 1) * SEQ], ACT.Copy,
                          scale=cols[:, norm_col + t:norm_col + t + 1]).then_inc(cn_hi_ready, 1)

                for u in (2, 3, 4, 5):
                    hi(U_LOW, u, 0, 0)
                slab_done(U_LOW, 3, 0, 0)
                sumsq(0)
                for u in (6, 7):
                    hi(U_LOW, u, 0, 0)
                hi_flat(U_LOW, 8, 0, 0, DC * 64)
                split_cn(0, PC_QN, cqT_hi)
                hi_flat(U_LOW, 9, 0, 0, DC * 64)
                slab_done(U_LOW, 7, 0, 0)
                sumsq(1)
                for k in range(2):
                    slab_done(U_LOW, 8 + k, 0, 0)
                    F(dk[:, k, :], ps[0:64, 0, k, 0:SEQ], ACT.Copy).then_inc(dk_copied, 1)
                    hi(U_ATT, k, 0, 0)
                    if k == 0:
                        split_cn(1, PC_KVN, ckT_hi)
                act.wait_ge(sp_x, 1)
                F(sp[3][:, :, :], sp[2][:, :, :], ACT.Exp).then_inc(sp_e, 1)
                act.wait_ge(kpe_turned, 1)
                F(kpeT[:, :], aux[:, 3, 0:SEQ], ACT.Copy).then_inc(kpe_read, 1)
            act.sem_inc(row_stored, 16)

            def ada2_bias(slab):
                act.wait_ge(row_stored, slab * 16 + 16)
                nc.scalar.dma_start(adarow[:, :], a["b_ada"][:, ds(slab * W + ADA1 * W, W)]).then_inc(bias_in, 16)

            def ada2_store(slab):
                act.wait_ge(row_ready, slab + 2)
                nc.scalar.dma_start(ada_rows[:, ds(slab * W, W)], adarow[:, :]).then_inc(row_stored, 16)

            if on("att"):
                with act.Fori(0, 4) as i:
                    hi(U_ATT, 2, i, N_ATT)
                    hi(U_ATT, 3, i, N_ATT)
                    ada2_bias(i)
                    slab_done(U_ATT, 1, i, N_ATT)
                    F(qn[:, 0:2, :].rearrange("p h t -> p (h t)"), ps[:, 1, 0, :], ACT.Copy)
                    F(qr[:, :, :, :].rearrange("p b h n -> p (b h n)"), ps[:, 0, 0, :], ACT.Copy).then_inc(qr_copied, 1)
                    hi(U_ATT, 4, i, N_ATT)
                    hi(U_ATT, 5, i, N_ATT)
                    slab_done(U_ATT, 3, i, N_ATT)
                    F(kn[:, 0:2, :].rearrange("p h t -> p (h t)"), aux[:, 2, :], ACT.Copy)
                    F(vt[:, 0, :], aux[:, 0, :], ACT.Copy).then_inc(att_evac_a, 1)
                    act.wait_ge(qpe_turned, i + 1)
                    F(qpeT[:, :, :].rearrange("p h t -> p (h t)"), ps[:, 1, 0, :], ACT.Copy).then_inc(qpe_read, 1)
                    hi(U_ATT, 6, i, N_ATT)
                    act.wait_ge(negmax_ready, i + 1)
                    for h in range(4):
                        for b in range(BLK):
                            c = slice(b * P, P + b * 2 * P)
                            last = F(probs[:, h, c], aux[:, h, c], ACT.Exp, bias=st[:, 8 + 4 * b + h:9 + 4 * b + h],
                                     scale=SCALE, accum_out=st[:, 16 + 4 * b + h:17 + 4 * b + h])
                    last.then_inc(exp_done, 1)
                    hi(U_ATT, 7, i, N_ATT)
                    hi(U_ATT, 8, i, N_ATT)
                    for h in (0, 2):
                        act.wait_ge(probs_turned, i * 4 + (h + 1))
                        F(pT[:, h, :], aux[:, h, 0:3 * P], ACT.Copy).then_inc(pT_a, 1)
                    hi(U_ATT, 9, i, N_ATT)
                    slab_done(U_ATT, 7, i, N_ATT)
                    for t in range(4):
                        last = F(premix[:, ds(i * 4 + t, 1), :].rearrange("p a t -> p (a t)"),
                                 ps[:, 0, t // 2, (t % 2) * SEQ:(t % 2) * SEQ + SEQ], ACT.Sigmoid,
                                 bias=cols[:, ds(i * 4 + (PC_BG + DC + t), 1)])
                    last.then_inc(b_free, 1)
                    act.wait_ge(pv_done, i + 1)
                    F(oT[:, ds(i * 4, 4), :], aux[:, :, 0:SEQ], ACT.Copy).then_inc(o_read, 1)
                    ada2_store(i)
            if on("mla"):
                act.wait_ge(o_read, 4)
                for q in range(4):
                    F(oT_hi[:, 4 * q:4 * q + 4, :], oT[:, 4 * q:4 * q + 4, :], ACT.Copy).then_inc(o_hi_ready, 1)
                act.wait_ge(cum_ready, 1)
                F(toend[:, :], aux[:, 2, 0:HEADS], ACT.Exp)
                F(fromst[:, :], aux[:, 2, HEADS:2 * HEADS], ACT.Exp).then_inc(decay_ready, 1)
                with act.Fori(0, 2) as i:
                    for s in range(2):
                        for q in range(4):
                            hi(U_MLA, 4 * s + q + 2, i, N_MLA)
                            if q == 1:
                                ada2_bias(i * 2 + (ADA_MLA + s))
                        ada2_store(i * 2 + (ADA_MLA + s))

            def store_y(number, tile):
                act.wait_ge(yt_turned, number)
                for t in range(4):
                    last = F(yT[:, ds(tile + t, 1), :].rearrange("p a t -> p (a t)"),
                             auxf[:, t * SEQ:(t + 1) * SEQ], ACT.Copy, scale=cols[:, ds(tile + (PC_NW + t), 1)])
                last.then_inc(yt_stored, 1)

            if on("ssd"):
                def ssd_pair(i, first):
                    for g in range(2):
                        u = 10 * g
                        grp = i * 2 + g

                        def decays(ks):
                            for k in ks:
                                act.wait_ge(diff_done, grp * 4 + (k + 3))
                                F(mt[:, k // 2, 4 * (k % 2):4 * (k % 2) + 4, :].rearrange("p h l -> p (h l)"),
                                  aux[:, 3 - k % 2, :], ACT.Exp).then_inc(decay_exp, 1)

                        for k in (2, 3, 4):
                            hi(U_SSD, u + k, i, N_SSD)
                            if k == 3 and not (first and g == 0):
                                ada2_store(grp + ADA_SSD - 1)
                        if not (first and g == 0):
                            store_y(grp, grp * 4 - 4)
                        decays((0, 1))
                        ada2_bias(grp + ADA_SSD)
                        hi(U_SSD, u + 5, i, N_SSD)
                        decays((2, 3))
                        hi(U_SSD, u + 6, i, N_SSD)
                        for t in range(4):
                            act.wait_ge(conv_done, grp * 6 + (t + 1))
                            F(xc[:, t, :], xc[:, t, :], ACT.Silu).then_inc(silu_done, 1)
                        hi(U_SSD, u + 7, i, N_SSD)
                        act.wait_ge(conv_done, grp * 6 + 6)
                        F(bcT[:, :, :], bcT[:, :, :], ACT.Silu).then_inc(silu_done, 1)
                        hi(U_SSD, u + 8, i, N_SSD)
                        act.wait_ge(xt_turned, grp + 1)
                        F(x_tok[:, :, :].rearrange("p b n -> p (b n)"), auxf[:, 0:1024], ACT.Copy).then_inc(xt_ready, 1)
                        for k in (9, 10, 11):
                            hi(U_SSD, u + k, i, N_SSD)
                        slab_done(U_SSD, u + 9, i, N_SSD)
                        F(zs[:, :, :], ps[:, 1 - g, :, :], ACT.Silu).then_inc(z_silu, 1)
                        act.wait_ge(yg_ready, grp + 1)
                        for b in range(BLK):
                            if b:
                                act.wait_ge(ysq_ready, grp * 2 + 1)
                            last = F(yjunk[:, :], yg[:, b, :], ACT.Square, accum_out=st[:, 40 + b:41 + b])
                            last.then_inc(ysq_ready, 1)
                        act.wait_ge(ysq_ready, grp * 2 + 2)
                        root(st[:, 42:44], st[:, 40:42], 1.0 / W)

                ssd_pair(0, True)
                with act.Fori(1, 4) as i:
                    ssd_pair(i, False)
                ada2_store(ADA_ALL - 1)

            if on("g0"):
                for s in range(4):
                    for q in range(4):
                        hi(U_G0, 4 * s + q + 2, 0, 0)
                    slab_done(U_G0, 4 * s + 3, 0, 0)
                    if s == 0:
                        act.wait_ge(row_stored, 16 * (ADA_ALL + 1))
                    for t in range(4):
                        last = F(g0[:, 4 * s + t, :], ps[:, 1 - s % 2, t // 2, (t % 2) * SEQ:(t % 2) * SEQ + SEQ],
                                 ACT.Sigmoid, bias=cols[:, PC_BG + 4 * s + t:PC_BG + 4 * s + t + 1])
                    last.then_inc(g0_ready, 1)
                    if s == 0:
                        store_y(GROUPS, 4 * (GROUPS - 1))
                        act.wait_ge(yt_stored, GROUPS)
                    F(yT_hi[:, 8 * s:8 * s + 8, :], yT[:, 8 * s:8 * s + 8, :], ACT.Copy).then_inc(yt_hi, 1)
            if on("so"):
                with act.Fori(0, 2) as i:
                    for u in range(16):
                        hi(U_SO, u + 2, i, N_SO)
            if on("mix"):
                act.wait_ge(pe_used, U_MIX + 2)
                for q in range(4):
                    act.wait_ge(premix_ready, 2 * q + 2)
                    F(mx_hi[:, 4 * q:4 * q + 4, :], premix[:, 4 * q:4 * q + 4, :], ACT.Copy).then_inc(mx_hi_ready, 1)
                with act.Fori(0, 2) as i:
                    for u in range(8):
                        hi(U_MIX, u + 2, i, N_MIX)
            if on("h2"):
                for n in range(2 * BLK):
                    if n < 2:
                        norm_root(n + 3, n)
                    if n == 1:
                        for b in range(BLK):
                            apply_norm(x1[:, b, :], x1[:, b, :], b, b + 1)
                    if n >= 2:
                        norm_root(n + 3, n - 2)
                        apply_norm(h2[:, n - 2, :], x1[:, n - 2, :], n - 2, n + 1)
                for b in range(BLK):
                    act.wait_ge(h2_turned, b + 1)
                    F(h2_hi[:, :, b * P:b * P + P], (auxf, psf)[b].rearrange("p (k t) -> p k t", t=P), ACT.Copy)\
                        .then_inc(h2_hi_ready, 1)
            if on("wq"):
                def score_out(s):
                    act.wait_ge(score_done, s + 1)
                    F(score[:, 2 * s:2 * s + 2, :].rearrange("p h k -> p (h k)"), aux[:, 2 * (s % 2), :], ACT.Copy)\
                        .then_inc(score_a, 1)

                for s in range(4):
                    for q in range(4):
                        if U_WQ + 4 * s + q + 2 < U_END:
                            hi(U_WQ, 4 * s + q + 2, 0, 0)
                        if s and q == 2:
                            score_out(s - 1)
                    slab_done(U_WQ, 4 * s + 3, 0, 0)
                    F(qT[:, 4 * s:4 * s + 2, :].rearrange("p k t -> p (k t)"), ps[:, 1 - s % 2, 0, :], ACT.Copy)\
                        .then_inc(qT_a, 1)
                score_out(3)
            if on("all"):
                act.wait_ge(score_v, 4)
                act.wait_ge(score_a, 4)
                for b in range(BLK):
                    if b:
                        act.wait_ge(row_used, ROWS + 2 * TOPK * PEER_HEADS * b)
                    F(auxf, h2[:, b, :], ACT.Copy).then_inc(h2_psum, 1)

                    def gate(n_expr, k):
                        act.wait_ge(top_ready, n_expr)
                        F(gex[:, k, :], tval[:, k, :], ACT.Exp, bias=ngm[:, k:k + 1], accum_out=gsum[:, k:k + 1])\
                            .then_inc(gate_exp, 1)

                    if b == 0:
                        gate(1, 0)

                    def pair(i, last_one):
                        for k in range(2):
                            act.wait_ge(row_used, i * (4 * TOPK) + (ROWS + (PEER_HEADS * b + k) * 2 * TOPK + TOPK))
                            F(gel[:, k, :], dots[:, k, :], ACT.Gelu).then_inc(gelu_ready, 1)
                            if not (last_one and k == 1):
                                gate(i * 2 + (PEER_HEADS * b + k + 2), 1 - k)

                    with act.Fori(0, 4 - b) as i:
                        pair(i, False)
                    if b:
                        pair(3, True)
                    norm_root(b + 7)

        @block.vector
        def _(dve):
            V = nc.vector
            S = Steps(dve, dve_step)
            link = S.link

            def lo(base, j, i, per, cols_=W):
                n = base + j
                dve.wait_ge(hi_ready, i * per + (n + 1))
                V.tensor_tensor(wlo[:, n % 2, :, 0:cols_], raw[:, n % 4, :, 0:cols_],
                                whi[:, n % 2, :, 0:cols_].bitcast(F32), ALU.subtract).then_inc(lo_ready, 1)

            def lo_flat(base, j, i, per, count):
                n = base + j
                dve.wait_ge(hi_ready, i * per + (n + 1))
                flat = lambda w: w.rearrange("p a b -> p (a b)")[:, 0:count]
                V.tensor_tensor(flat(wlo[:, n % 2]), flat(raw[:, n % 4]), flat(whi[:, n % 2]).bitcast(F32),
                                ALU.subtract).then_inc(lo_ready, 1)

            def slab_done(base, j, i, per):
                dve.wait_ge(pe_used, i * per + (base + j + 3))

            def rsqrt(cols_, number):
                dve.wait_ge(std_ready, number)
                link(V.reciprocal(cols_, cols_))

            def stats(src, b=0):
                for k in range(4):
                    S.step(V.bn_stats(bn[:, b, k, :], src[:, k * W:(k + 1) * W]))

            def moments(b=0):
                S.wait()
                V.bn_aggr(st[:, 44 + 4 * b:46 + 4 * b], bn[:, b].rearrange("p a b -> p (a b)")).then_inc(var_ready, 1)

            def normalise(dst, src, number):
                stats(src)
                moments()
                rsqrt(st[:, 46:47], number)
                return V.tensor_scalar(dst, src, st[:, 44:45], st[:, 46:47], ALU.subtract, ALU.mult)

            def offset(b, number):
                rsqrt(st[:, 46 + 4 * b:47 + 4 * b], number)
                V.scalar_tensor_tensor(st[:, 47 + 4 * b:48 + 4 * b], st[:, 44 + 4 * b:45 + 4 * b], -1.0,
                                       st[:, 46 + 4 * b:47 + 4 * b], ALU.mult, ALU.mult).then_inc(offset_ready, 1)

            dve.sem_inc(lo_ready, 4)
            dve.sem_inc(ada_used, 4)
            dve.sem_inc(ada2_used, 4)
            dve.sem_inc(ada3_used, 2)
            dve.sem_inc(row_ready, 1)
            dve.sem_inc(row_used, ROWS)
            dve.wait_ge(rows_turned, 1)
            V.tensor_copy(cols[:, :], aux[:, 0, 0:COLS_ALL]).then_inc(cols_ready, 1)
            dve.wait_ge(rows_turned, 2)
            V.tensor_copy(keysT[:, :, :].rearrange("p a b -> p (a b)"), aux[:, 1, 0:2 * KEYS]).then_inc(cols_ready, 1)
            dve.wait_ge(c_ready, 1)

            def ada_rows_in(acc_, tile, k0, count, used=None):
                for kc in range(count):
                    k = k0 + kc
                    if k == 0:
                        last = V.tensor_scalar(acc_, tile[:, kc, :], csil[:, k:k + 1], None, ALU.mult)
                    else:
                        last = V.scalar_tensor_tensor(acc_, tile[:, kc, :], csil[:, k:k + 1], acc_, ALU.mult, ALU.add)
                    if k < DC - 1:
                        link(last)
                return last

            def ada1_slab(k):
                dve.wait_ge(acc_summed, k + 1)
                for q in range(4):
                    dve.wait_ge(ada_full[q], 16 * (k + 1))
                    last = ada_rows_in(acc[:, k % 2, :], ada_in[:, q], 4 * q, 4)
                    if q < 3:
                        dve.sem_inc(ada_used, 1)
                last.then_inc(acc_ready, 1)
                dve.wait_ge(acc_ready, k + 1)
                dve.sem_inc(ada_used, 1)

            ada1_slab(0)
            dve.wait_ge(x_loaded, 16 * BLK)
            for b in range(BLK):
                normalise(x_in[:, b, :], x_in[:, b, :], b + 1).then_inc(x_normed, 1)
            link(V.tensor_copy(posf[:, :], posi[:, :]))
            for b in range(BLK):
                S.step(V.tensor_scalar(ang[:, b, :], con[:, C_FREQ:C_FREQ + 32], posf[:, b:b + 1], None, ALU.mult))
            S.wait()
            c1 = 6.28125
            c2 = float(np.float32(np.round((2 * math.pi - c1) * 2 ** 21) / 2 ** 21))
            c3 = float(np.float32(2 * math.pi - c1 - c2))
            for k in range(2):
                link(V.tensor_scalar(turn[:, :, :], ang[:, :, :], 1 / (2 * math.pi), 0.25 * k, ALU.mult, ALU.add))
                link(V.tensor_scalar(turn[:, :, :], turn[:, :, :], 12582912.0, None, ALU.add))
                link(V.tensor_scalar(turn[:, :, :], turn[:, :, :], 12582912.0, None, ALU.subtract))
                src = ang
                for c in (c1, c2, c3):
                    link(V.scalar_tensor_tensor(angs[:, k], turn[:, :, :], -c, src[:, :, :] if src is ang else src,
                                                ALU.mult, ALU.add))
                    src = angs[:, k]
                link(V.tensor_scalar(angs[:, k], angs[:, k], k * math.pi / 2, 3.1415925, ALU.add, ALU.min))
                last = V.tensor_scalar(angs[:, k], angs[:, k], -3.1415925, None, ALU.max)
                S.step(last) if k == 0 else last.then_inc(angles_ready, 1)

            for k in range(1, ADA1):
                ada1_slab(k)
            dve.wait_ge(acc_summed, ADA1 + 2)
            link(V.tensor_tensor(adacol[:, :], ps[:, 1, 1, 0:2 * DC], cols[:, PC_ADA:PC_ADA + 2 * DC], ALU.add))
            link(V.tensor_scalar(adacol[:, DC:2 * DC], adacol[:, DC:2 * DC], 1.0, None, ALU.add))
            dve.wait_ge(xT_ready, 4)

            def h_low_part(q):
                dve.wait_ge(h_hi_ready, q + 1)
                V.tensor_tensor(h_lo[:, 4 * q:4 * q + 4, :], xnT[:, 4 * q:4 * q + 4, :],
                                h_hi[:, 4 * q:4 * q + 4, :].bitcast(F32), ALU.subtract).then_inc(h_ready, 1)

            for q in range(4):
                for k in range(4 * q, 4 * q + 4):
                    last = V.tensor_scalar(xnT[:, k, :], xnT[:, k, :], adacol[:, DC + k:DC + k + 1],
                                           adacol[:, k:k + 1], ALU.mult, ALU.add)
                    S.step(last) if k % 4 < 3 else last.then_inc(h_full, 1)
                if q:
                    h_low_part(q - 1)
                if q == 1:
                    lo(U_LOW, 0, 0, 0)
            h_low_part(3)
            lo(U_LOW, 1, 0, 0)

            def ada2(slab, q, in_ssd=False):
                if q == 0:
                    dve.wait_ge(acc_summed, slab + (ADA1 + 2))
                for e in range(2):
                    j = 2 * q + e
                    if in_ssd:
                        dve.wait_ge(ada3_full[e], (slab - ADA_SSD) * 64 + 16 * (q + 1))
                    else:
                        dve.wait_ge(ada2_full[j % 4], slab * 32 + 16 * (j // 4 + 1))
                    last = ada_rows_in(acc[:, 0, :], ada2_in[:, 2 + e if in_ssd else j % 4], 4 * q + 2 * e, 2)
                    if j == 7:
                        last.then_inc(acc_ready, 1)
                        dve.wait_ge(acc_ready, slab + (ADA1 + 1))
                    dve.sem_inc(ada3_used if in_ssd else ada2_used, 1)

            def ada2_row(bank, slab):
                dve.wait_ge(bias_in, slab * 16 + 16)
                dve.wait_ge(acc_summed, slab + (ADA1 + 3))
                V.tensor_tensor(adarow[:, :], bank[0:1, :], adarow[:, :], ALU.add).then_inc(row_ready, 1)

            if on("low"):
                def rms(s):
                    rsqrt(st[:, 36 + 2 * s:38 + 2 * s], s + 3)
                    if s:
                        dve.wait_ge(cn_turned, s)
                    for b in range(BLK):
                        last = V.tensor_scalar(cn[:, b, :], ps[:, s, b, :], st[:, 36 + 2 * s + b:37 + 2 * s + b],
                                               None, ALU.mult)
                        S.step(last) if b == 0 else last.then_inc(cn_ready, 1)

                def split_cn(s, norm_col, dst_hi, dst_lo):
                    for t in range(RC):
                        dve.wait_ge(cn_hi_ready, RC * s + (t | 1) + 1)
                        last = V.scalar_tensor_tensor(
                            dst_lo[:, t, :], auxf[:, 1024 * s + t * SEQ:1024 * s + (t + 1) * SEQ],
                            cols[:, norm_col + t:norm_col + t + 1], dst_hi[:, t, :].bitcast(F32),
                            ALU.mult, ALU.subtract)
                        S.step(last) if t < RC - 1 else last.then_inc(cn_split, 1)

                for u in (2, 3, 4, 5):
                    lo(U_LOW, u, 0, 0)
                slab_done(U_LOW, 3, 0, 0)
                rms(0)
                for u in (6, 7):
                    lo(U_LOW, u, 0, 0)
                lo_flat(U_LOW, 8, 0, 0, DC * 64)
                split_cn(0, PC_QN, cqT_hi, cqT_lo)
                lo_flat(U_LOW, 9, 0, 0, DC * 64)
                slab_done(U_LOW, 7, 0, 0)
                rms(1)
                lo(U_ATT, 0, 0, 0)
                split_cn(1, PC_KVN, ckT_hi, ckT_lo)
                lo(U_ATT, 1, 0, 0)
                dve.wait_ge(dk_turned, 2)
                bc = dtb[:, :].unsqueeze(1).broadcast_to([P, BLK, HEADS])
                link(V.tensor_tensor(sp[0][:, :, :], aux[:, 0:2, 0:HEADS], bc, ALU.add))
                link(V.tensor_scalar(sp[1][:, :, :], sp[0][:, :, :], -1.0, None, ALU.mult))
                V.tensor_tensor(sp[2][:, :, :], sp[0][:, :, :], sp[1][:, :, :], ALU.min).then_inc(sp_x, 1)
                dve.wait_ge(sines_ready, 4)
                S.step(V.tensor_tensor(krt[:, :, :], aux[:, 0:2, 64:128], cos2[:, :, :], ALU.mult))
                V.tensor_tensor(krs[:, :, :], aux[:, 0:2, 64:128], sin2[:, :, :], ALU.mult).then_inc(b_free, 1)
                dve.wait_ge(b_free, 1)
                S.wait()
                for e in range(2):
                    S.step(V.tensor_tensor(kpe2[:, :, e, 0:32], krt[:, :, 0:32], krs[:, :, 32:64], ALU.subtract))
                    last = V.tensor_tensor(kpe2[:, :, e, 32:64], krs[:, :, 0:32], krt[:, :, 32:64], ALU.add)
                    S.step(last) if e == 0 else last.then_inc(kpe_ready, 1)
                dve.wait_ge(sp_e, 1)
                s0, s1, s2, s3, s4, s5 = (t[:, :, :] for t in sp)
                link(V.tensor_scalar(s4, s3, 2.0, None, ALU.add))
                link(V.reciprocal(s5, s4))
                link(V.tensor_tensor(s4, s3, s5, ALU.mult))
                link(V.tensor_tensor(s5, s4, s4, ALU.mult))
                link(V.tensor_scalar(s1, s5, 1 / 17, None, ALU.mult))
                for k in (15, 13, 11, 9, 7, 5, 3):
                    link(V.scalar_tensor_tensor(s1, s1, 1 / k, s5, ALU.add, ALU.mult))
                link(V.scalar_tensor_tensor(s1, s1, 1.0, s4, ALU.add, ALU.mult))
                link(V.tensor_scalar(s2, s0, 0.0, None, ALU.max))
                link(V.scalar_tensor_tensor(dtv[:, :, :], s1, 2.0, s2, ALU.mult, ALU.add))
                dve.wait_ge(neg_a, 1)
                V.scalar_tensor_tensor(adt[:, :, :], dtv[:, :, :], -1.0,
                                       anegA[:, :].unsqueeze(1).broadcast_to([P, BLK, HEADS]),
                                       ALU.mult, ALU.mult).then_inc(adt_ready, 1)
            if on("att"):
                cosb, sinb = (t[:, :, :].unsqueeze(2).broadcast_to([P, BLK, 4, ROPE]) for t in (cos2, sin2))
                with dve.Fori(0, 4) as i:
                    S.enter(i, 9 + DC - 1)
                    lo(U_ATT, 2, i, N_ATT)
                    lo(U_ATT, 3, i, N_ATT)
                    slab_done(U_ATT, 1, i, N_ATT)
                    S.step(V.tensor_copy(qn[:, 2:4, :].rearrange("p h t -> p (h t)"), ps[:, 1, 1, :]))
                    dve.wait_ge(qr_copied, i + 1)
                    for b in range(BLK):
                        S.step(V.tensor_tensor(qrt[:, b], qr[:, b], cosb[:, b], ALU.mult))
                        S.step(V.tensor_tensor(qrs[:, b], qr[:, b], sinb[:, b], ALU.mult))
                    S.wait()
                    S.step(V.tensor_tensor(qr[:, :, :, 0:32], qrt[:, :, :, 0:32], qrs[:, :, :, 32:64], ALU.subtract))
                    V.tensor_tensor(qr[:, :, :, 32:64], qrs[:, :, :, 0:32], qrt[:, :, :, 32:64], ALU.add)\
                        .then_inc(qr_ready, 1)
                    lo(U_ATT, 4, i, N_ATT)
                    lo(U_ATT, 5, i, N_ATT)
                    slab_done(U_ATT, 3, i, N_ATT)
                    V.tensor_copy(kn[:, 2:4, :].rearrange("p h t -> p (h t)"), aux[:, 3, :])
                    V.tensor_copy(vt[:, 1, :], aux[:, 1, :]).then_inc(att_evac_v, 1)
                    ada2(i, 0)
                    lo(U_ATT, 6, i, N_ATT)
                    dve.wait_ge(scores_done, i + 1)
                    for b in range(BLK):
                        S.step(V.tensor_reduce(st[:, 4 * b:4 * b + 4], aux[:, :, b * P:P + b * 2 * P], AX_X, ALU.max))
                    S.wait()
                    V.tensor_scalar(st[:, 8:16], st[:, 0:8], -SCALE, None, ALU.mult).then_inc(negmax_ready, 1)
                    ada2(i, 1)
                    dve.wait_ge(exp_done, i + 1)
                    link(V.reciprocal(st[:, 24:32], st[:, 16:24]))
                    for b in range(BLK):
                        c = slice(b * P, P + b * 2 * P)
                        last = V.tensor_tensor(probs[:, :, c], probs[:, :, c],
                                               st[:, 24 + 4 * b:28 + 4 * b].unsqueeze(2).broadcast_to([P, 4, P * (b + 1)]),
                                               ALU.mult)
                        if b:
                            last.then_inc(probs_ready, 1)
                    lo(U_ATT, 7, i, N_ATT)
                    ada2(i, 2)
                    lo(U_ATT, 8, i, N_ATT)
                    for h in (1, 3):
                        dve.wait_ge(probs_turned, i * 4 + (h + 1))
                        V.tensor_copy(pT[:, h, :], aux[:, h, 0:3 * P]).then_inc(pT_v, 1)
                    ada2(i, 3)
                    lo(U_ATT, 9, i, N_ATT)
                    ada2_row(ps[:, 1, 1, :], i)
                S.leave(4)
            if on("mla"):
                for q in range(4):
                    dve.wait_ge(o_hi_ready, q + 1)
                    V.tensor_tensor(oT_lo[:, 4 * q:4 * q + 4, :], oT[:, 4 * q:4 * q + 4, :],
                                    oT_hi[:, 4 * q:4 * q + 4, :].bitcast(F32), ALU.subtract).then_inc(o_split, 1)
                dve.wait_ge(b_free, 5)
                with dve.Fori(0, 2) as i:
                    S.enter(i, 4 + 2 * (DC - 1))
                    for s in range(2):
                        slab = i * 2 + (ADA_MLA + s)
                        for q in range(4):
                            ada2(slab, q)
                            lo(U_MLA, 4 * s + q + 2, i, N_MLA)
                        slab_done(U_MLA, 4 * s + 3, i, N_MLA)
                        for k in range(2):
                            m = premix[:, ds(i * 8 + (4 * s + 2 * k), 2), :]
                            S.step(V.tensor_tensor(m, ps[:, 1 - s, k, :].rearrange("p (k t) -> p k t", t=SEQ), m,
                                                   ALU.mult))
                        ada2_row(aux[:, 0, :], slab)
                S.leave(2)
            if on("ssd"):
                SSD_STEPS = 25 + DC - 1

                def ssd_pair(i, first):
                    for g in range(2):
                        u = 10 * g
                        grp = i * 2 + g
                        slab = grp + ADA_SSD
                        lo(U_SSD, u + 2, i, N_SSD)
                        lo(U_SSD, u + 3, i, N_SSD)
                        ada2(slab, 0, True)
                        lo(U_SSD, u + 4, i, N_SSD)
                        ada2(slab, 1, True)
                        lo(U_SSD, u + 5, i, N_SSD)

                        def conv(tiles):
                            for dst, src, tile in tiles:
                                S.step(V.tensor_scalar(dst, src, cols[:, ds(tile + PC_CW[3], 1)],
                                                       cols[:, ds(tile + PC_CB, 1)], ALU.mult, ALU.add))
                            for j in (2, 1, 0):
                                s = 3 - j
                                for t, (dst, src, tile) in enumerate(tiles):
                                    S.wait(len(tiles) - 1 - (t if j == 0 else 0))
                                    last = V.scalar_tensor_tensor(dst[:, s:SEQ], src[:, 0:SEQ - s],
                                                                  cols[:, ds(tile + PC_CW[j], 1)], dst[:, s:SEQ],
                                                                  ALU.mult, ALU.add)
                                    S.step(last) if j else last.then_inc(conv_done, 1)

                        slab_done(U_SSD, u + 3, i, N_SSD)
                        conv([(xc[:, t, :], ps[:, 1 - g, t // 2, (t % 2) * SEQ:(t % 2) * SEQ + SEQ],
                               i * 8 + (4 * g + t)) for t in range(4)])
                        lo(U_SSD, u + 6, i, N_SSD)
                        slab_done(U_SSD, u + 4, i, N_SSD)
                        conv([(bcT[:, 0, :], ps[:, g, 0, 0:SEQ], i * 2 + (32 + g))])
                        lo(U_SSD, u + 7, i, N_SSD)
                        slab_done(U_SSD, u + 5, i, N_SSD)
                        conv([(bcT[:, 1, :], ps[:, g, 1, 0:SEQ], i * 2 + (40 + g))])
                        lo(U_SSD, u + 8, i, N_SSD)
                        ada2(slab, 2, True)
                        lo(U_SSD, u + 9, i, N_SSD)
                        dve.wait_ge(cb_done, grp + 1)
                        S.step(V.tensor_tensor(cbm[:, 0:2, :], aux[:, 2, 0:2 * P].rearrange("p (k l) -> p k l", l=P),
                                               upper.unsqueeze(1).broadcast_to([P, 2, P]), ALU.mult))
                        V.tensor_copy(cbm[:, 2, :], aux[:, 2, 2 * P:3 * P]).then_inc(cb_read, 1)
                        S.wait()
                        for k in range(4):
                            dve.wait_ge(decay_exp, grp * 4 + (k + 1))
                            m = mt[:, k // 2, 4 * (k % 2):4 * (k % 2) + 4, :]
                            V.tensor_tensor(m, m, cbm[:, k // 2, :].unsqueeze(1).broadcast_to([P, 4, P]), ALU.mult)\
                                .then_inc(mt_ready, 1)
                        lo(U_SSD, u + 10, i, N_SSD)
                        ada2(slab, 3, True)
                        lo(U_SSD, u + 11, i, N_SSD)
                        dve.wait_ge(y_done, grp + 1)
                        dve.wait_ge(xskip_ready, grp + 1)
                        y1 = yg[:, 1, :]
                        link(V.tensor_tensor(y1.rearrange("p (h d) -> p h d", d=HD),
                                             aux[:, 3, :].rearrange("p (h d) -> p h d", d=HD),
                                             fromst[:, ds(i * 2 * HG + g * HG, HG)].unsqueeze(2).broadcast_to([P, HG, HD]),
                                             ALU.mult))
                        link(V.tensor_tensor(y1, y1, aux[:, 1, :], ALU.add))
                        S.step(V.tensor_tensor(y1, y1, x_tok[:, 1, :], ALU.add))
                        S.step(V.tensor_tensor(yg[:, 0, :], aux[:, 0, :], x_tok[:, 0, :], ALU.add))
                        S.wait()
                        dve.wait_ge(z_silu, grp + 1)
                        V.tensor_tensor(yg[:, :, :], yg[:, :, :], zs[:, :, :], ALU.mult).then_inc(yg_ready, 1)
                        ada2_row(aux[:, 2, :], slab)
                        rsqrt(st[:, 42:44], grp + 5)
                        for b in range(BLK):
                            last = V.tensor_scalar(yg[:, b, :], yg[:, b, :], st[:, 42 + b:43 + b], None, ALU.mult)
                            S.step(last) if b == 0 else last.then_inc(ytok_ready, 1)
                            if b == 0:
                                S.wait()

                ssd_pair(0, True)
                with dve.Fori(1, 4) as i:
                    S.enter(i, 2 * SSD_STEPS, 1)
                    ssd_pair(i, False)
                S.leave(3)
            if on("g0"):
                for s in range(4):
                    for q in range(4):
                        lo(U_G0, 4 * s + q + 2, 0, 0)
                    dve.wait_ge(yt_hi, s + 1)
                    y8 = slice(8 * s, 8 * s + 8)
                    V.tensor_tensor(yT_lo[:, y8, :], yT[:, y8, :], yT_hi[:, y8, :].bitcast(F32), ALU.subtract)\
                        .then_inc(yt_split, 1)
            if on("so"):
                dve.wait_ge(g0_ready, 4)
                with dve.Fori(0, 2) as i:
                    S.enter(i, 4)
                    for s in range(2):
                        for q in range(8):
                            lo(U_SO, 8 * s + q + 2, i, N_SO)
                        slab_done(U_SO, 8 * s + 7, i, N_SO)
                        for k in range(2):
                            m = ds(i * 8 + (4 * s + 2 * k), 2)
                            gt = gtmp[:, :].rearrange("p (k t) -> p k t", t=SEQ)
                            link(V.tensor_tensor(gt, ps[:, 1 - s, k, :].rearrange("p (k t) -> p k t", t=SEQ),
                                                 g0[:, m, :], ALU.mult))
                            V.tensor_tensor(premix[:, m, :], premix[:, m, :], gt, ALU.add).then_inc(premix_ready, 1)
                            dve.wait_ge(premix_ready, i * 4 + (2 * s + k + 1))
                S.leave(2)
            if on("mix"):
                for q in range(4):
                    dve.wait_ge(mx_hi_ready, q + 1)
                    V.tensor_tensor(mx_lo[:, 4 * q:4 * q + 4, :], premix[:, 4 * q:4 * q + 4, :],
                                    mx_hi[:, 4 * q:4 * q + 4, :].bitcast(F32), ALU.subtract).then_inc(mx_split, 1)
                dve.wait_ge(res_in, 16 * 4)
                dve.wait_ge(ada_in_ready, 16 * 4)
                with dve.Fori(0, 2) as i:
                    S.enter(i, 12)
                    for s in range(2):
                        for q in range(4):
                            lo(U_MIX, 4 * s + q + 2, i, N_MIX)
                        slab_done(U_MIX, 4 * s + 3, i, N_MIX)
                        c = ds(i * 2 * W + s * W, W)
                        for b in range(BLK):
                            link(V.scalar_tensor_tensor(mtmp[:, :], gate1[:, c], 1.0, ps[:, 1 - s, b, :],
                                                        ALU.add, ALU.mult))
                            link(V.scalar_tensor_tensor(x1[:, b, c], x1[:, b, c], ALPHA, mtmp[:, :],
                                                        ALU.mult, ALU.add))
                            S.step(V.bn_stats(bn[:, b, ds(i * 2 + s, 1), :].rearrange("p a n -> p (a n)"),
                                              x1[:, b, c]))
                S.leave(2)
            if on("h2"):
                for b in range(BLK):
                    moments(b)
                for b in range(BLK):
                    offset(b, 13 + b)
                dve.wait_ge(normed, 1)
                link(V.tensor_tensor(x1[:, 0, :], x1[:, 0, :], ln1[:, 0, :], ALU.mult))
                link(V.tensor_tensor(x1[:, 0, :], x1[:, 0, :], ln1[:, 1, :], ALU.add))
                stats(x1[:, 0, :], 0)
                moments(0)
                offset(0, 15)

                def modulate(b):
                    dve.wait_ge(normed, 3 + b)
                    link(V.scalar_tensor_tensor(h2[:, b, :], scale2, 1.0, h2[:, b, :], ALU.add, ALU.mult))
                    V.tensor_tensor(h2[:, b, :], h2[:, b, :], shift2, ALU.add).then_inc(h2_ready, 1)

                modulate(0)
                dve.wait_ge(x1_ready, 2)
                stats(x1[:, 1, :], 1)
                moments(1)
                offset(1, 16)
                modulate(1)
                for b in range(BLK):
                    dve.wait_ge(h2_hi_ready, b + 1)
                    V.tensor_tensor(h2_lo[:, :, b * P:b * P + P], (auxf, psf)[b].rearrange("p (k t) -> p k t", t=P),
                                    h2_hi[:, :, b * P:b * P + P].bitcast(F32), ALU.subtract).then_inc(h2_split, 1)
            if on("wq"):
                NEG = -3.0e38
                iota = con[:, C_IOTA:C_IOTA + TOPK]

                def top16(vals, idx, src, work):
                    dve.sem_inc(held, 1)
                    link(V.max(vals[:, 0:8], src))
                    dve.sem_inc(held, 1)
                    link(V.max_index(idx[:, 0:8], vals[:, 0:8], src))
                    dve.sem_inc(held, 1)
                    link(V.match_replace(work, vals[:, 0:8], src, NEG))
                    dve.sem_inc(held, 1)
                    link(V.max(vals[:, 8:16], work))
                    dve.sem_inc(held, 1)
                    link(V.max_index(idx[:, 8:16], vals[:, 8:16], work))

                def top_sides(head):
                    link(V.tensor_copy(scur[:, :, :].rearrange("p a b -> p (a b)"),
                                       score[:, ds(head, 1), :].rearrange("p a b -> p (a b)")))
                    for s in range(2):
                        top16(sval[:, s, :], sidx[:, s, :], scur[:, s, :], swork[:, s, :])

                def top_pairs(k):
                    link(V.tensor_copy(sidf[:, :, :], sidx[:, :, :]))
                    link(V.tensor_tensor(cand[:, :, :], sval[:, 0, :].unsqueeze(2).broadcast_to([P, TOPK, TOPK]),
                                         sval[:, 1, :].unsqueeze(1).broadcast_to([P, TOPK, TOPK]), ALU.add))
                    top16(tval[:, k, :], tpos, cand[:, :, :].rearrange("p a b -> p (a b)"), cwork[:, :])

                def top_experts(k):
                    S.step(V.tensor_scalar(tab[:, 0, :], tpos[:, :], 4, None, ALU.logical_shift_right))
                    link(V.tensor_scalar(tab[:, 1, :], tpos[:, :], 15, None, ALU.bitwise_and))
                    link(V.tensor_copy(tabf[:, :, :], tab[:, :, :]))
                    for s in range(2):
                        link(V.tensor_tensor(onehot[:, :, :], tabf[:, s, :].unsqueeze(2).broadcast_to([P, TOPK, TOPK]),
                                             iota.unsqueeze(1).broadcast_to([P, TOPK, TOPK]), ALU.is_equal))
                        link(V.tensor_tensor(onehot[:, :, :], onehot[:, :, :],
                                             sidf[:, s, :].unsqueeze(1).broadcast_to([P, TOPK, TOPK]), ALU.mult))
                        link(V.tensor_reduce(tsel[:, s, :], onehot[:, :, :], AX_X, ALU.add))
                    link(V.scalar_tensor_tensor(eidf[:, :], tsel[:, 0, :], float(KEYS), tsel[:, 1, :], ALU.mult, ALU.add))
                    V.tensor_copy(eid[:, k, :], eidf[:, :]).then_inc(expert_ready, 1)
                    V.tensor_scalar(ngm[:, k:k + 1], tval[:, k, 0:1], -1.0, None, ALU.mult).then_inc(top_ready, 1)

                def use_row(r0, e, n_trip):
                    r = r0 + e
                    dve.wait_ge(row_full[r % ROWS], n_trip * (16 * 4 * TOPK // ROWS) + 16 * (r // ROWS + 1))
                    return rrow[:, r % ROWS, :]

                def score_out(s):
                    dve.wait_ge(score_done, s + 1)
                    h0 = PEER_HEADS + 2 * s
                    V.tensor_copy(score[:, h0:h0 + 2, :].rearrange("p h k -> p (h k)"), aux[:, 2 * (s % 2) + 1, :])\
                        .then_inc(score_v, 1)

                for s in range(4):
                    for q in range(4):
                        if U_WQ + 4 * s + q + 2 < U_END:
                            lo(U_WQ, 4 * s + q + 2, 0, 0)
                        if s and q == 2:
                            score_out(s - 1)
                        if (s, q) == (2, 0):
                            dve.wait_ge(score_a, 1)
                            top_sides(0)
                        if (s, q) == (2, 2):
                            top_pairs(0)
                        if (s, q) == (3, 0):
                            top_experts(0)
                    slab_done(U_WQ, 4 * s + 3, 0, 0)
                    V.tensor_copy(qT[:, 4 * s + 2:4 * s + 4, :].rearrange("p k t -> p (k t)"), ps[:, 1 - s % 2, 1, :])\
                        .then_inc(qT_v, 1)
                score_out(3)
            if on("all"):
                dve.wait_ge(ln2_in, 32)
                dve.wait_ge(qT_a, 4)
                for b in range(BLK):
                    link(V.memset(psf, 0.0))
                    dve.wait_ge(h2_psum, b + 1)
                    dve.wait_ge(score_a, 4)
                    base = b * PEER_HEADS * 2 * TOPK

                    def pair(i, last_one, i_sem):
                        for k in range(2):
                            r0 = base + k * 2 * TOPK
                            for e in range(TOPK):
                                row = use_row(r0, e, i_sem)
                                last = V.tensor_tensor_reduce(row, row, auxf, 1.0, 0.0, ALU.mult, ALU.add,
                                                              dots[:, k, e:e + 1])
                                last.then_inc(row_used, 1)
                            if not (last_one and k == 1):
                                top_sides(i * 2 + (PEER_HEADS * b + k + 1))
                                top_pairs(1 - k)
                                top_experts(1 - k)
                            dve.wait_ge(gate_exp, i_sem * 2 + (PEER_HEADS * b + k + 1))
                            link(V.reciprocal(st[:, 48 + k:49 + k], gsum[:, k:k + 1]))
                            dve.wait_ge(gelu_ready, i_sem * 2 + (PEER_HEADS * b + k + 1))
                            link(V.scalar_tensor_tensor(wgt[:, k, :], gel[:, k, :], st[:, 48 + k:49 + k],
                                                        gex[:, k, :], ALU.mult, ALU.mult))
                            for e in range(TOPK):
                                row = use_row(r0 + TOPK, e, i_sem)
                                if e:
                                    dve.wait_ge(row_used, i_sem * (4 * TOPK) + (ROWS + r0 + TOPK + e))
                                V.scalar_tensor_tensor(psf, row, wgt[:, k, e:e + 1], psf, ALU.mult, ALU.add)\
                                    .then_inc(row_used, 1)

                    with dve.Fori(0, 4 - b) as i:
                        S.enter(i, 2 * 30)
                        pair(i, False, i)
                    S.leave(4 - b)
                    if b:
                        pair(3, True, 3)
                    dve.wait_ge(row_used, ROWS + base + PEER_HEADS * 2 * TOPK)
                    if b:
                        dve.wait_ge(out_done, 16)
                    link(V.scalar_tensor_tensor(fin[:, :], gate2, 1.0, psf, ALU.add, ALU.mult))
                    link(V.scalar_tensor_tensor(fin[:, :], x1[:, b, :], ALPHA, fin[:, :], ALU.mult, ALU.add))
                    link(normalise(fin[:, :], fin[:, :], 17 + b))
                    link(V.tensor_tensor(fin[:, :], fin[:, :], ln2[:, 0, :], ALU.mult))
                    V.tensor_tensor(fin[:, :], fin[:, :], ln2[:, 1, :], ALU.add).then_inc(fin_ready, 1)

        @block.gpsimd
        def _(pool):
            G = nc.gpsimd
            S = Steps(pool, pool_step)

            def ada2(slab, q, in_ssd=False):
                for e in range(2):
                    j = 2 * q + e
                    if in_ssd:
                        pool.wait_ge(ada3_used, (slab - ADA_SSD) * 8 + (j + 1))
                    else:
                        pool.wait_ge(ada2_used, slab * 8 + (j + 1))
                    G.dma_start(ada2_in[:, 2 + e if in_ssd else j % 4],
                                w_ada[:, 2 * j:2 * j + 2, ds(slab * W + ADA1 * W, W)])\
                        .then_inc(ada3_full[e] if in_ssd else ada2_full[j % 4], 16)

            if on("att"):
                pool.wait_ge(lo_ready, 5)
                with pool.Fori(0, 8 if on("mla") else 4) as i:
                    for q in range(4):
                        ada2(i, q)
            if on("ssd"):
                pool.wait_ge(ada2_used, 4 + 8 * ADA_SSD)
                pool.wait_ge(decay_ready, 1)
                pool.wait_ge(params_in, 16 * 18)
                pool.wait_ge(pe_used, U_SSD + 2)
                with pool.Fori(0, 4) as i:
                    S.enter(i, 4)
                    for g in range(2):
                        grp = i * 2 + g
                        ada2(grp + ADA_SSD, 0, True)
                        hd = i * 2 * HG + g * HG
                        for k in range(4):
                            if k == 2:
                                ada2(grp + ADA_SSD, 1, True)
                            pool.wait_ge(diff_done, grp * 4 + (k + 1))
                            G.tensor_tensor(rad[:, k % 2, :, :], upper.unsqueeze(1).broadcast_to([P, 4, P]),
                                            adt[:, k // 2, ds(hd + 4 * (k % 2), 4)].unsqueeze(2).broadcast_to([P, 4, P]),
                                            ALU.mult).then_inc(rad_ready, 1)
                        ada2(grp + ADA_SSD, 2, True)
                        pool.wait_ge(xt_ready, grp + 1)
                        v3 = lambda t: t.rearrange("p (h d) -> p h d", d=HD)
                        per_head = lambda t: t.unsqueeze(2).broadcast_to([P, HG, HD])
                        for b in range(BLK):
                            S.step(G.tensor_tensor(v3(xdt[:, b, :]), v3(x_tok[:, b, :]),
                                                   per_head(dtv[:, b, ds(hd, HG)]), ALU.mult))
                        S.wait()
                        G.tensor_tensor(v3(xend[:, :]), v3(xdt[:, 0, :]), per_head(toend[:, ds(hd, HG)]), ALU.mult)\
                            .then_inc(xdt_ready, 1)
                        for b in range(BLK):
                            last = G.tensor_tensor(v3(x_tok[:, b, :]), v3(x_tok[:, b, :]),
                                                   per_head(dskip[:, ds(hd, HG)]), ALU.mult)
                            if b:
                                last.then_inc(xskip_ready, 1)
                        ada2(grp + ADA_SSD, 3, True)
                S.leave(4)
            if on("mix"):
                pool.wait_ge(pe_used, U_SO + 2)
                pool.wait_ge(row_stored, 16 * (ADA_ALL + 1))
                for k in range(4):
                    G.dma_start(adabc[:, k, :], ada_rows[:, k * D:(k + 1) * D].broadcast_to([P, D]))\
                        .then_inc(ada_in_ready, 16)
                pool.wait_ge(premix_ready, 8)
                for b in range(BLK):
                    G.dma_start(x1[:, b, :], a["x"][0, b * P:(b + 1) * P, :]).then_inc(res_in, 16)
                for k, n in enumerate(("ln1_g", "ln1_b")):
                    G.dma_start(ln1[:, k, :], a[n].broadcast_to([P, D])).then_inc(res_in, 16)
            if on("h2"):
                pool.wait_ge(res_in, 16 * 4)
                pool.wait_ge(normed, 2)
                G.tensor_tensor(x1[:, 1, :], x1[:, 1, :], ln1[:, 0, :], ALU.mult).then_inc(x1_ready, 1)
                pool.wait_ge(x1_ready, 1)
                G.tensor_tensor(x1[:, 1, :], x1[:, 1, :], ln1[:, 1, :], ALU.add).then_inc(x1_ready, 1)
            if on("all"):
                pool.wait_ge(h2_ready, BLK)
                for k, n in enumerate(("ln2_g", "ln2_b")):
                    G.dma_start(ln2[:, k, :], a[n].broadcast_to([P, D])).then_inc(ln2_in, 16)
                for b in range(BLK):
                    base = b * PEER_HEADS * 2 * TOPK

                    def pair(i):
                        for k in range(2):
                            pool.wait_ge(expert_ready, i * 2 + (PEER_HEADS * b + k + 1))
                            for s, table in enumerate(("peer_u", "peer_v")):
                                for e in range(TOPK):
                                    r = base + (2 * k + s) * TOPK + e
                                    if b == 0 and r in (0, 1):
                                        pool.wait_ge(lo_ready, U_END + 3 + r)
                                    if b == 0 and r == 4:
                                        pool.wait_ge(pe_used, U_END + 2)
                                    pool.wait_ge(row_used, i * (4 * TOPK) + (r + 1))
                                    pool.sem_inc(held, 1)
                                    G.indirect_dma_start(
                                        out=rrow[:, r % ROWS, :], out_offset=None, in_=a[table][0],
                                        in_offset=bass.IndirectOffsetOnAxis(ap=eid[:, k, e:e + 1], axis=0))\
                                        .then_inc(row_full[r % ROWS], 16)

                    with pool.Fori(0, 4) as i:
                        pair(i)

    return nc


INPUTS = ("x", "c", "positions", "w_ada", "b_ada", "w_in", "b_gate", "conv_w", "conv_b", "dt_bias", "A_log", "D_skip",
          "ssd_norm_w", "w_ssd_out", "q_norm_w", "w_uq", "kv_norm_w", "w_ukv", "w_mla_out", "w_mix_out",
          "ln1_g", "ln1_b", "peer_w_q", "peer_keys_1", "peer_keys_2", "peer_u", "peer_v", "ln2_g", "ln2_b")


def kernel(**inputs):
    import concourse.bacc as bacc
    from concourse.bass_utils import run_bass_kernel_spmd

    nc = bacc.Bacc("TRN2", target_bir_lowering=False, num_devices=1)
    arrays, aps = {}, {}
    for name in INPUTS + ("consts",):
        x = constants() if name == "consts" else np.ascontiguousarray(inputs[name])
        arrays[f"in_{name}"] = x
        aps[name] = nc.dram_tensor(f"in_{name}", x.shape, mybir.dt.from_np(x.dtype), kind="ExternalInput").ap()
    out = nc.dram_tensor("out", (1, SEQ, D), F32, kind="ExternalOutput").ap()
    build(nc, aps, out)
    result = run_bass_kernel_spmd(nc, [arrays], core_ids=[0])
    return result.results[0]["out"]
```
